# Optimizing a Trainium2 kernel written in Bass

```python
import jax
import jax.numpy as jnp
from jax import lax
import numpy as np

D_MODEL = 1024
BATCH = 1
SEQ = 256
DEPTH = 2

N_MEM = 256
EPS = 1e-6
Q_BLOCK = 128
FFN_DIM = 2816

A_HEADS = 4
A_Q_LORA = 384
A_KV_LORA = 256
A_NOPE = 128
A_ROPE = 64
A_V = 128
ROPE_BASE = 10000.0

B_HEADS = 4
B_HEAD_DIM = 128
B_WIDTH = B_HEADS * B_HEAD_DIM
B_CONV = 4
B_CHUNK = 128

C_HEADS = 8
C_Q_LORA = 384
C_KV_LORA = 256
C_NOPE = 128
C_V = 128
IDX_HEADS = 8
IDX_DIM = 64
TOPK_MAX = 256

X_HEADS = 4
X_HEAD_DIM = 128

AB_IN = A_Q_LORA + A_KV_LORA + A_ROPE + 3 * B_WIDTH
AB_SPLITS = (A_Q_LORA, A_Q_LORA + A_KV_LORA, A_Q_LORA + A_KV_LORA + A_ROPE,
             A_Q_LORA + A_KV_LORA + A_ROPE + B_WIDTH, A_Q_LORA + A_KV_LORA + A_ROPE + 2 * B_WIDTH)
AB_MIX = A_HEADS * A_V + B_WIDTH
C_IN = C_Q_LORA + C_KV_LORA + IDX_HEADS * IDX_DIM + IDX_DIM + IDX_HEADS
C_SPLITS = (C_Q_LORA, C_Q_LORA + C_KV_LORA, C_Q_LORA + C_KV_LORA + IDX_HEADS * IDX_DIM,
            C_Q_LORA + C_KV_LORA + IDX_HEADS * IDX_DIM + IDX_DIM)
N_EVEN = (DEPTH + 1) // 2
N_ODD = DEPTH // 2

kernel_name = 'hybrid_mla_mlstm_dsa_macaron'

def rmsnorm(x, g):
    xf = x.astype(jnp.float32)
    y = xf * lax.rsqrt(jnp.mean(xf * xf, -1, keepdims=True) + EPS)
    return (y * g.astype(jnp.float32)).astype(x.dtype)

def swiglu(x, wg, wu, wd):
    return (jax.nn.silu(x @ wg) * (x @ wu)) @ wd

def rope(x, positions):
    half = x.shape[-1] // 2
    inv = ROPE_BASE ** (-jnp.arange(half, dtype=jnp.float32) / half)
    ang = positions.astype(jnp.float32)[..., None] * inv
    ang = ang.reshape(ang.shape[:2] + (1,) * (x.ndim - 3) + (half,))
    cos, sin = jnp.cos(ang), jnp.sin(ang)
    xf = x.astype(jnp.float32)
    x1, x2 = xf[..., :half], xf[..., half:]
    return jnp.concatenate([x1 * cos - x2 * sin, x1 * sin + x2 * cos], -1).astype(x.dtype)

def causal_block_attention(q, k, v, scale):
    seq = q.shape[2]
    tri = jnp.tril(jnp.ones((Q_BLOCK, Q_BLOCK), bool))
    outs = []
    for i0 in range(0, seq, Q_BLOCK):
        end = i0 + Q_BLOCK
        s = jnp.einsum('bhqd,bhkd->bhqk', q[:, :, i0:end], k[:, :, :end]).astype(jnp.float32) * scale
        mask = jnp.concatenate([jnp.ones((Q_BLOCK, i0), bool), tri], axis=1)
        p = jax.nn.softmax(jnp.where(mask, s, -jnp.inf), axis=-1).astype(v.dtype)
        outs.append(jnp.einsum('bhqk,bhkd->bhqd', p, v[:, :, :end]))
    return jnp.concatenate(outs, axis=2)

def mla_mixer(cq, ckv, kr, positions, cq_g, ckv_g, w_uq, w_ukv):
    b, s, _ = cq.shape
    q = (rmsnorm(cq, cq_g) @ w_uq).reshape(b, s, A_HEADS, A_NOPE + A_ROPE)
    q_nope, q_rope = q[..., :A_NOPE], rope(q[..., A_NOPE:], positions)
    kv = (rmsnorm(ckv, ckv_g) @ w_ukv).reshape(b, s, A_HEADS, A_NOPE + A_V)
    k_nope, v = kv[..., :A_NOPE], kv[..., A_NOPE:]
    k_rope = jnp.broadcast_to(rope(kr, positions)[:, :, None, :], (b, s, A_HEADS, A_ROPE))
    qf = jnp.concatenate([q_nope, q_rope], -1).transpose(0, 2, 1, 3)
    kf = jnp.concatenate([k_nope, k_rope], -1).transpose(0, 2, 1, 3)
    o = causal_block_attention(qf, kf, v.transpose(0, 2, 1, 3), (A_NOPE + A_ROPE) ** -0.5)
    return o.transpose(0, 2, 1, 3).reshape(b, s, A_HEADS * A_V)

def causal_dwconv(x, w, bias):
    y = lax.conv_general_dilated(x, w[:, None, :], window_strides=(1,), padding=[(B_CONV - 1, 0)],
                                 dimension_numbers=('NWC', 'WIO', 'NWC'), feature_group_count=x.shape[-1])
    return y + bias

def mlstm_chunkwise(q, k, v, li, lf):
    b, h, s, d = q.shape
    nc = s // B_CHUNK

    def to_chunks(t):
        return jnp.moveaxis(t.reshape((b, h, nc, B_CHUNK) + t.shape[3:]), 2, 0)

    causal = jnp.tril(jnp.ones((B_CHUNK, B_CHUNK), bool))

    def step(carry, inp):
        c_st, n_st, m_st = carry
        qj, kj, vj, lij, lfj = inp
        bcum = jnp.cumsum(lfj, -1)
        dmat = bcum[..., :, None] - bcum[..., None, :] + lij[..., None, :]
        dmat = jnp.where(causal, dmat, -jnp.inf)
        m_inter = bcum + m_st[..., None]
        m_j = jnp.maximum(m_inter, jnp.max(dmat, -1))
        sc = jnp.einsum('bhld,bhsd->bhls', qj, kj) * jnp.exp(dmat - m_j[..., None])
        inter = jnp.exp(m_inter - m_j)
        num = inter[..., None] * jnp.einsum('bhld,bhdv->bhlv', qj, c_st) + jnp.einsum('bhls,bhsv->bhlv', sc, vj)
        den = inter * jnp.einsum('bhld,bhd->bhl', qj, n_st) + jnp.sum(sc, -1)
        hj = num / jnp.maximum(jnp.abs(den), jnp.exp(-m_j))[..., None]
        b_tot = bcum[..., -1]
        g = b_tot[..., None] - bcum + lij
        m_new = jnp.maximum(b_tot + m_st, jnp.max(g, -1))
        decay = jnp.exp(b_tot + m_st - m_new)
        wg = jnp.exp(g - m_new[..., None])
        c_new = decay[..., None, None] * c_st + jnp.einsum('bhs,bhsd,bhsv->bhdv', wg, kj, vj)
        n_new = decay[..., None] * n_st + jnp.einsum('bhs,bhsd->bhd', wg, kj)
        return (c_new, n_new, m_new), hj

    init = (jnp.zeros((b, h, d, d), jnp.float32), jnp.zeros((b, h, d), jnp.float32),
            jnp.zeros((b, h), jnp.float32))
    _, hs = lax.scan(step, init, (to_chunks(q), to_chunks(k), to_chunks(v), to_chunks(li), to_chunks(lf)))
    return jnp.moveaxis(hs, 0, 2).reshape(b, h, s, d)

def mlstm_mixer(xm, vm, og, conv_w, conv_b, wq, wk, w_gates, b_gates, gn_g, skip):
    b, s, _ = xm.shape
    xc = jax.nn.silu(causal_dwconv(xm, conv_w, conv_b))
    xch = xc.reshape(b, s, B_HEADS, B_HEAD_DIM)
    q = jnp.einsum('bshd,hde->bshe', xch, wq)
    k = jnp.einsum('bshd,hde->bshe', xch, wk)
    gates = (jnp.concatenate([q.reshape(b, s, B_WIDTH), k.reshape(b, s, B_WIDTH), vm], -1) @ w_gates
             + b_gates).astype(jnp.float32)
    li = gates[..., :B_HEADS]
    lf = jax.nn.log_sigmoid(gates[..., B_HEADS:])
    to_bhs = lambda t: jnp.moveaxis(t.astype(jnp.float32), 2, 1)
    hh = mlstm_chunkwise(to_bhs(q), to_bhs(k) * B_HEAD_DIM ** -0.5,
                         to_bhs(vm.reshape(b, s, B_HEADS, B_HEAD_DIM)), to_bhs(li), to_bhs(lf))
    mu = jnp.mean(hh, -1, keepdims=True)
    var = jnp.mean(jnp.square(hh - mu), -1, keepdims=True)
    hn = ((hh - mu) * lax.rsqrt(var + EPS)).transpose(0, 2, 1, 3).reshape(b, s, B_WIDTH)
    out = ((hn * gn_g.astype(jnp.float32) + skip.astype(jnp.float32) * xc.astype(jnp.float32))
           * jax.nn.sigmoid(og.astype(jnp.float32)))
    return out.astype(xm.dtype)

def dsa_mixer(h, w_in, cq_g, ckv_g, w_uq, w_uk, w_uv):
    b, s, _ = h.shape
    cq, ckv, qi, ki, wi = jnp.split(h @ w_in, C_SPLITS, axis=-1)
    q = (rmsnorm(cq, cq_g) @ w_uq).reshape(b, s, C_HEADS, C_NOPE)
    ckv = rmsnorm(ckv, ckv_g)
    q_lat = jnp.einsum('bshd,hcd->bshc', q, w_uk)
    qi = qi.reshape(b, s, IDX_HEADS, IDX_DIM)
    topk = min(TOPK_MAX, s // 4)
    scale = C_NOPE ** -0.5
    outs = []
    for i0 in range(0, s, Q_BLOCK):
        end = i0 + Q_BLOCK
        kk = min(topk, end)
        t_pos = jnp.arange(i0, end)
        admissible = jnp.arange(end)[None, :] <= t_pos[:, None]
        rel = jax.nn.relu(jnp.einsum('bthd,bsd->bths', qi[:, i0:end], ki[:, :end]))
        score = jnp.einsum('bths,bth->bts', rel, wi[:, i0:end]).astype(jnp.float32)
        _, idx = lax.top_k(jnp.where(admissible, score, -jnp.inf), kk)
        valid = idx <= t_pos[None, :, None]
        c_sel = jax.vmap(lambda c, i: c[i])(ckv[:, :end], idx)
        logits = jnp.einsum('bthc,btkc->bthk', q_lat[:, i0:end], c_sel).astype(jnp.float32) * scale
        p = jax.nn.softmax(jnp.where(valid[:, :, None, :], logits, -jnp.inf), -1).astype(c_sel.dtype)
        outs.append(jnp.einsum('bthk,btkc->bthc', p, c_sel))
    o_lat = jnp.concatenate(outs, 1)
    return jnp.einsum('bshc,hcv->bshv', o_lat, w_uv).reshape(b, s, C_HEADS * C_V)

def memory_cross_attention(h, mem_n, wq, wk, wv, wo):
    b, s, _ = h.shape
    q = (h @ wq).reshape(b, s, X_HEADS, X_HEAD_DIM)
    k = (mem_n @ wk).reshape(b, -1, X_HEADS, X_HEAD_DIM)
    v = (mem_n @ wv).reshape(b, -1, X_HEADS, X_HEAD_DIM)
    logits = jnp.einsum('bshd,bmhd->bhsm', q, k).astype(jnp.float32) * X_HEAD_DIM ** -0.5
    p = jax.nn.softmax(logits, -1).astype(v.dtype)
    return jnp.einsum('bhsm,bmhd->bshd', p, v).reshape(b, s, X_HEADS * X_HEAD_DIM) @ wo

def setup_inputs(seed: int = 0) -> dict:
    key = jax.random.key(seed)
    ks = iter(jax.random.split(key, 64))
    f32 = jnp.float32
    nrm = lambda shape, fan_in: jax.random.normal(next(ks), shape, f32) * fan_in ** -0.5
    gain = lambda shape: 1.0 + 0.05 * jax.random.normal(next(ks), shape, f32)
    small = lambda shape: 0.02 * jax.random.normal(next(ks), shape, f32)
    x = jax.random.normal(next(ks), (BATCH, SEQ, D_MODEL), f32)
    mem = jax.random.normal(next(ks), (BATCH, N_MEM, D_MODEL), f32)
    positions = (jax.random.randint(next(ks), (BATCH, 1), 0, 1024, jnp.int32)
                 + jnp.arange(SEQ, dtype=jnp.int32)[None, :])
    b_gates = jnp.concatenate([
        0.1 * jax.random.normal(next(ks), (N_EVEN, B_HEADS), f32),
        jnp.linspace(3.0, 6.0, B_HEADS, dtype=f32)[None, :]
        + 0.1 * jax.random.normal(next(ks), (N_EVEN, B_HEADS), f32)], axis=-1)
    return {
        'x': x,
        'mem': mem,
        'positions': positions,
        'norm_g': gain((DEPTH, 8, D_MODEL)),
        'mem_norm_g': gain((DEPTH, D_MODEL)),
        'ffn_w_gate': nrm((DEPTH, 2, D_MODEL, FFN_DIM), D_MODEL),
        'ffn_w_up': nrm((DEPTH, 2, D_MODEL, FFN_DIM), D_MODEL),
        'ffn_w_down': nrm((DEPTH, 2, FFN_DIM, D_MODEL), FFN_DIM),
        'xa_wq': nrm((DEPTH, D_MODEL, X_HEADS * X_HEAD_DIM), D_MODEL),
        'xa_wk': nrm((DEPTH, D_MODEL, X_HEADS * X_HEAD_DIM), D_MODEL),
        'xa_wv': nrm((DEPTH, D_MODEL, X_HEADS * X_HEAD_DIM), D_MODEL),
        'xa_wo': nrm((DEPTH, X_HEADS * X_HEAD_DIM, D_MODEL), X_HEADS * X_HEAD_DIM),
        'ab_w_in': nrm((N_EVEN, D_MODEL, AB_IN), D_MODEL),
        'ab_w_out': nrm((N_EVEN, AB_MIX, D_MODEL), AB_MIX),
        'mla_cq_g': gain((N_EVEN, A_Q_LORA)),
        'mla_ckv_g': gain((N_EVEN, A_KV_LORA)),
        'mla_w_uq': nrm((N_EVEN, A_Q_LORA, A_HEADS * (A_NOPE + A_ROPE)), A_Q_LORA),
        'mla_w_ukv': nrm((N_EVEN, A_KV_LORA, A_HEADS * (A_NOPE + A_V)), A_KV_LORA),
        'ml_conv_w': nrm((N_EVEN, B_CONV, B_WIDTH), B_CONV),
        'ml_conv_b': small((N_EVEN, B_WIDTH)),
        'ml_wq': nrm((N_EVEN, B_HEADS, B_HEAD_DIM, B_HEAD_DIM), B_HEAD_DIM),
        'ml_wk': nrm((N_EVEN, B_HEADS, B_HEAD_DIM, B_HEAD_DIM), B_HEAD_DIM),
        'ml_w_gates': nrm((N_EVEN, 3 * B_WIDTH, 2 * B_HEADS), 3 * B_WIDTH),
        'ml_b_gates': b_gates,
        'ml_gn_g': gain((N_EVEN, B_WIDTH)),
        'ml_skip': gain((N_EVEN, B_WIDTH)),
        'c_w_in': nrm((N_ODD, D_MODEL, C_IN), D_MODEL),
        'c_w_out': nrm((N_ODD, C_HEADS * C_V, D_MODEL), C_HEADS * C_V),
        'c_cq_g': gain((N_ODD, C_Q_LORA)),
        'c_ckv_g': gain((N_ODD, C_KV_LORA)),
        'c_w_uq': nrm((N_ODD, C_Q_LORA, C_HEADS * C_NOPE), C_Q_LORA),
        'c_w_uk': nrm((N_ODD, C_HEADS, C_KV_LORA, C_NOPE), C_KV_LORA),
        'c_w_uv': nrm((N_ODD, C_HEADS, C_KV_LORA, C_V), C_KV_LORA),
    }

def reference(x, mem, positions, norm_g, mem_norm_g, ffn_w_gate, ffn_w_up, ffn_w_down,
              xa_wq, xa_wk, xa_wv, xa_wo, ab_w_in, ab_w_out, mla_cq_g, mla_ckv_g, mla_w_uq, mla_w_ukv,
              ml_conv_w, ml_conv_b, ml_wq, ml_wk, ml_w_gates, ml_b_gates, ml_gn_g, ml_skip,
              c_w_in, c_w_out, c_cq_g, c_ckv_g, c_w_uq, c_w_uk, c_w_uv):
    for l in range(DEPTH):
        g = norm_g[l]
        h = rmsnorm(x, g[0])
        x = x + 0.5 * rmsnorm(swiglu(h, ffn_w_gate[l, 0], ffn_w_up[l, 0], ffn_w_down[l, 0]), g[1])
        h = rmsnorm(x, g[2])
        if l % 2 == 0:
            e = l // 2
            cq, ckv, kr, xm, vm, og = jnp.split(h @ ab_w_in[e], AB_SPLITS, axis=-1)
            ya = mla_mixer(cq, ckv, kr, positions, mla_cq_g[e], mla_ckv_g[e], mla_w_uq[e], mla_w_ukv[e])
            yb = mlstm_mixer(xm, vm, og, ml_conv_w[e], ml_conv_b[e], ml_wq[e], ml_wk[e],
                             ml_w_gates[e], ml_b_gates[e], ml_gn_g[e], ml_skip[e])
            y = jnp.concatenate([ya, yb], axis=-1) @ ab_w_out[e]
        else:
            o = l // 2
            y = dsa_mixer(h, c_w_in[o], c_cq_g[o], c_ckv_g[o], c_w_uq[o], c_w_uk[o], c_w_uv[o]) @ c_w_out[o]
        x = x + rmsnorm(y, g[3])
        h = rmsnorm(x, g[4])
        y = memory_cross_attention(h, rmsnorm(mem, mem_norm_g[l]), xa_wq[l], xa_wk[l], xa_wv[l], xa_wo[l])
        x = x + rmsnorm(y, g[5])
        h = rmsnorm(x, g[6])
        x = x + 0.5 * rmsnorm(swiglu(h, ffn_w_gate[l, 1], ffn_w_up[l, 1], ffn_w_down[l, 1]), g[7])
    return x


_drawn_inputs = setup_inputs


def setup_inputs(seed=0):
    import zlib

    import numpy as np

    out = dict(_drawn_inputs(seed))
    spreads = {}
    factors = {'c_cq_g': 5.4}
    for name, (base, spread) in spreads.items():
        noise = np.random.default_rng([zlib.crc32(name.encode()), seed]).standard_normal(out[name].shape)
        drawn = base * np.exp(spread * noise) if base else spread * noise
        out[name] = jnp.asarray(drawn.astype(out[name].dtype))
    for name, factor in factors.items():
        out[name] = (out[name] * factor).astype(out[name].dtype)
    return out
```

```python
import numpy as np
import concourse.bass as bass
from concourse import mybir
from contextlib import ExitStack

F32, F32R, I32 = mybir.dt.float32, mybir.dt.float32r, mybir.dt.int32
ALU, ACT, AX = mybir.AluOpType, mybir.ActivationFunctionType, mybir.AxisListType

P = 128
TOK, D, L = 256, 1024, 2
NT, KT = TOK // P, D // P
FF = 2816
PAIRS = FF // (2 * P)
EPS = 1e-6
HD = 128
ROPE, HALF = 64, 32
QL, KVL = 384, 256
BW = 512
NEG = -1.0e30
TAKEN = -3.0e38
TOPK = 64
SUBS = 4 * L
CH = 2048
RING = 3
BANKS = 4

INS = ['x', 'mem', 'positions', 'norm_g', 'mem_norm_g', 'ffn_w_gate', 'ffn_w_up', 'ffn_w_down', 'xa_wq', 'xa_wk',
       'xa_wv', 'xa_wo', 'ab_w_in', 'ab_w_out', 'mla_cq_g', 'mla_ckv_g', 'mla_w_uq', 'mla_w_ukv', 'ml_conv_w',
       'ml_conv_b', 'ml_wq', 'ml_wk', 'ml_w_gates', 'ml_b_gates', 'ml_gn_g', 'ml_skip', 'c_w_in', 'c_w_out',
       'c_cq_g', 'c_ckv_g', 'c_w_uq', 'c_w_uk', 'c_w_uv']



def weight_chunks(A):
    out = []

    def cols(w, c0, c1):
        return w[:, c0:c1].rearrange("(k p) n -> p k n", p=P)

    def add(name, src, split=True, down=False):
        out.append((name, src, split, down))

    def ffn(s):
        l, j = s // 4, (s % 4) // 2
        g, u, d = A['ffn_w_gate'][l, j], A['ffn_w_up'][l, j], A['ffn_w_down'][l, j]

        def up(p):
            add(f"G{s}.{p}", cols(g, 2 * P * p, 2 * P * (p + 1)))
            add(f"U{s}.{p}", cols(u, 2 * P * p, 2 * P * (p + 1)))
        up(0)
        for p in range(PAIRS):
            if p + 1 < PAIRS:
                up(p + 1)
            add(f"D{s}.{p}", d[2 * P * p:2 * P * (p + 1)].rearrange("(k p) n -> p k n", p=P), down=True)

    def rows(name, w):
        for i in range(w.shape[0] // (2 * P)):
            add(f"{name}.{i}", w[2 * P * i:2 * P * (i + 1)].rearrange("(k p) n -> p k n", p=P), down=True)

    def memory_kv(l, *names):
        for n, i in names:
            add(f"x{n}{l}.{i}", cols(A[f'xa_w{n}'][l], 256 * i, 256 * (i + 1)))

    def cross(l):
        for i in range(2):
            add(f"xq{l}.{i}", cols(A['xa_wq'][l], 256 * i, 256 * (i + 1)))
        rows(f"xo{l}", A['xa_wo'][l])

    ffn(0)
    w = A['ab_w_in'][0]
    for name, c0, c1 in AB_COLS[:8]:
        add(name, cols(w, c0, c1))
    for i in range(2):
        add(f"uq.{i}", cols(A['mla_w_uq'][0], 384 * i, 384 * (i + 1)), split=False)
    add("ukv", cols(A['mla_w_ukv'][0], 0, 1024), split=False)
    add("og.1", cols(w, *AB_COLS[8][1:]))
    memory_kv(0, ("k", 0), ("k", 1), ("v", 0))
    add("mwq", A['ml_wq'][0].rearrange("h p n -> p h n"), split=False)
    add("mwk", A['ml_wk'][0].rearrange("h p n -> p h n"), split=False)
    memory_kv(0, ("v", 1))
    rows("abo", A['ab_w_out'][0])
    cross(0)
    ffn(3)
    ffn(4)
    for name, c0, c1 in C_COLS:
        add(name, cols(A['c_w_in'][0], c0, c1))
    for i in range(2):
        add(f"cuq.{i}", cols(A['c_w_uq'][0], 512 * i, 512 * (i + 1)), split=False)
    for n in ("uk", "uv"):
        for i in range(2):
            add(f"c{n}_{i}", A[f'c_w_{n}'][0, 4 * i:4 * (i + 1)].rearrange("h (k p) n -> p (h k) n", p=P), split=False)
    memory_kv(1, ("k", 0), ("k", 1), ("v", 0), ("v", 1))
    rows("co", A['c_w_out'][0])
    cross(1)
    ffn(7)
    return out


AB_COLS = [("ab.0", 0, 256), ("ab.1", 256, 512), ("ab.2", 512, 704), ("xm.0", 704, 960), ("xm.1", 960, 1216),
           ("vm.0", 1216, 1472), ("vm.1", 1472, 1728), ("og.0", 1728, 1984), ("og.1", 1984, 2240)]
C_COLS = [("c.0", 0, 256), ("c.1", 256, 512), ("c.2", 512, 640), ("qi.0", 640, 896), ("qi.1", 896, 1152),
          ("kw", 1152, 1224)]

UNITS = [("mla", t, i) for i in range(2) for t in range(NT)]
UNITS += [("xa0", t, i) for i in range(2) for t in range(NT)]
UNITS += [("dsa", t, i) for i in range(4) for t in range(NT)]
UNITS += [("xa1", t, i) for i in range(2) for t in range(NT)]
FILL = {"mla": ["og.1", "xk0.0", "xk0.1", "xv0.0"], "dsa": ["xk1.0", "xk1.1", "xv1.0", "xv1.1"]}


def units_of(key):
    return [u for u, unit in enumerate(UNITS) if unit[0] == key]


def bank_uses():
    out = []

    def pre(n):
        out.extend(f"h{n}.{k}" for k in range(KT // 2))

    def ffn(s):
        out.extend(f"{w}{s}.{p}" for p in range(PAIRS) for w in "GU")

    def attention(key, fill=()):
        us = units_of(key)
        out.append(f"score{us[0]}")
        for n, u in enumerate(us):
            if n + 1 < len(us):
                out.append(f"score{us[n + 1]}")
            if n:
                out.append(f"pv{us[n - 1]}")
            if n < len(fill):
                out.append(fill[n])
            out.append(f"pT{u}")
        out.append(f"pv{us[-1]}")

    out.append("gains")
    pre("m")
    pre(0)
    ffn(0)
    pre(1)
    out.extend(n for n, _, _ in AB_COLS[:8])
    out.extend(["cqT.0", "cqT.1", "ckvT"])
    out.extend(["uqn.0", "uqr.0", "uqn.1", "uqr.1", "kT.0", "kT.1", "v.0", "v.1"])
    out.extend(["vmT.0", "vmT.1", "rT.0", "rT.1"])
    attention("mla", FILL["mla"])
    out.extend(["mq.0", "mq.1", "mk.0", "mk.1", "ktok", "gates", "xv0.1", "cum", "arow.0", "arow.1", "S.0", "S.1",
                "state.0", "state.1", "scT.0", "scT.1", "qc.0", "qc.1", "num0.0", "num0.1", "num1.0", "num1.1",
                "hnT.0", "hnT.1"])
    pre(2)
    out.extend(["xq0.0", "xq0.1"])
    attention("xa0")
    pre(3)
    ffn(3)
    pre(4)
    ffn(4)
    pre(5)
    out.extend(n for n, _, _ in C_COLS)
    out.extend(["ccqT.0", "ccqT.1", "cckvT", "kiT"])
    out.extend(f"rel{t}.{i}" for t in range(NT) for i in range(4))
    out.extend(f"cuq.{i}.{j}" for i in range(2) for j in range(2))
    out.extend(f"cuk.{i}" for i in range(4))
    out.extend(f"cuv.{i}.{t}" for i in range(2) for t in range(NT))
    attention("dsa", FILL["dsa"])
    pre(6)
    out.extend(["xq1.0", "xq1.1"])
    attention("xa1")
    pre(7)
    ffn(7)
    return out


NORMS = ["m", "pre0", "post0", "pre1", "cq", "ckv", "post1", "pre2", "post2", "pre3", "post3", "pre4", "post4",
         "pre5", "ccq", "cckv", "post5", "pre6", "post6", "pre7", "post7"]
NORM_WIDTH = {"cq": QL, "ccq": QL, "ckv": KVL, "cckv": KVL}
FFNS = {0: 0, 3: 1, 4: 2, 7: 3}

LAST_USE = {"uq.0": "uqr.0", "uq.1": "uqr.1", "ukv": "v.1", "mwq": "mq.1", "mwk": "ktok", "cuq.0": "cuq.0.1",
            "cuq.1": "cuq.1.1", "cuk_0": "cuk.1", "cuk_1": "cuk.3", "cuv_0": "cuv.0.1",
            "cuv_1": "cuv.1.1"}


def build(nc, A, out):
    ctx = ExitStack()
    with ctx:
        def sb(name, shape, dt=F32):
            return ctx.enter_context(nc.sbuf_tensor(name, shape, dt))

        def sem(name):
            return ctx.enter_context(nc.semaphore(name))

        raw = sb("raw", [P, RING, CH])
        w_hi = sb("w_hi", [P, RING, CH], F32R)
        w_lo = sb("w_lo", [P, RING, CH], F32R)
        x = sb("x_state", [P, NT, D])
        h_hi = sb("h_hi", [P, KT, TOK], F32R)
        h_lo = sb("h_lo", [P, KT, TOK], F32R)
        m_hi = sb("m_hi", [P, KT, TOK], F32R)
        m_lo = sb("m_lo", [P, KT, TOK], F32R)
        memT = sb("memT", [P, KT, TOK])
        gain_row = sb("gain_row", [P, D])
        QT = sb("QT", [P, 8, TOK])
        KTs = sb("KTs", [P, 8, TOK])
        V = sb("V", [P, 2, NT, 512])
        XK = sb("XK", [P, 4, TOK])
        XV = sb("XV", [P, NT, 512])
        work = sb("work", [P, 3200])
        lat = sb("lat", [P, NT, QL + KVL])
        latT = sb("latT", [P, 5, TOK])
        qrT = sb("qrT", [P, 2, TOK])
        krT = sb("krT", [P, NT, TOK])
        xmT = sb("xmT", [P, 4, TOK + 3])
        xcT = sb("xcT", [P, 4, TOK])
        vaug = sb("vaug", [P, NT, 4, HD + 1])
        ogT = sb("ogT", [P, 4, TOK])
        ident = sb("ident", [P, P])
        ones = sb("ones", [P, P])
        upper = sb("upper", [P, P])
        cmask = sb("cmask", [P, NT, TOK])
        gcol = sb("gcol", [P, P])
        pcol = sb("pcol", [P, 64])
        w_gates = sb("w_gates", [P, 12, 8])
        b_gates = sb("b_gates", [P, 8])
        pos_i = sb("pos_i", [P, NT], I32)
        pos = sb("pos", [P, NT])
        inv_freq = sb("inv_freq", [P, HALF])
        turns_i = sb("turns_i", [P, NT, HALF], I32)
        ang = sb("ang", [P, 4, NT, HALF])
        cos = sb("cos", [P, NT, HALF])
        sin = sb("sin", [P, NT, HALF])
        NN = len(NORMS)
        ss = sb("ss", [P, NN, NT])
        ms = sb("ms", [P, NN, NT])
        rstd = sb("rstd", [P, NN, NT])
        minus_half = sb("minus_half", [P, 8])
        U = len(UNITS)
        nmax = sb("nmax", [P, U, 2])
        esum = sb("esum", [P, U, 2])
        einv = sb("einv", [P, U, 2])
        iw = sb("iw", [P, NT, 8])
        top8 = sb("top8", [P, NT, 8])
        gts = sb("gts", [P, NT, 8])
        small = sb("small", [P, 24, 8])

        psum = ctx.enter_context(nc.psum_tensor("psum", [P, 8, 512], F32))
        y = psum[:, 0:4, :].rearrange("p (t a) n -> p t (a n)", t=NT)

        xn = QT[:, :, :].rearrange("p a b -> p (a b)").rearrange("p (t n) -> p t n", t=NT)
        stage = KTs[:, :, :].rearrange("p a b -> p (a b)").rearrange("p (t n) -> p t n", t=NT)
        Vf = V[:, :, :, :].rearrange("p a b c -> p (a b c)")
        junk = Vf.rearrange("p (t n) -> p t n", t=NT)
        sg = Vf[:, 0:1024].rearrange("p (a n) -> p a n", a=2)
        gu = Vf[:, 1024:2048].rearrange("p (a n) -> p a n", a=2)
        g_hi = m_hi[:, 0:4, :].rearrange("p (a b) n -> p a b n", a=2)
        g_lo = m_lo[:, 0:4, :].rearrange("p (a b) n -> p a b n", a=2)
        s_sb = work[:, 0:1024].rearrange("p (a h n) -> p a h n", a=2, h=2)
        p_sb = work[:, 1024:2048].rearrange("p (a h n) -> p a h n", a=2, h=2)
        pT = work[:, 2048:3072].rearrange("p (a h k n) -> p a h k n", a=2, h=2, k=2)
        grow, prow = work[:, 0:P], work[0:64, P:2 * P]
        rin = work[:, 0:640].rearrange("p (t h n) -> p t h n", t=NT, h=5)
        rout = work[:, 640:1664].rearrange("p (t h n) -> p t h n", t=NT, h=8)
        rtmp = work[:, 1664:2304].rearrange("p (a t h n) -> p a t h n", a=2, t=NT, h=5)
        vmT = V[:, 1, :, :].rearrange("p a b -> p (a b)").rearrange("p (h n) -> p h n", h=4)
        mqT, mkT = QT[:, 4:8, :], KTs[:, 4:8, :]
        Dm = work[:, 0:1024].rearrange("p (t h n) -> p t h n", t=NT, h=4)
        nd = work[:, 0:1032].rearrange("p (t h n) -> p t h n", t=NT, h=4)
        dga = work[:, 1032:2056].rearrange("p (t h n) -> p t h n", t=NT, h=4)
        sc = dga
        qcs = work[:, 1032:1548].rearrange("p (h n) -> p h n", h=4)
        sq = work[:, 1032:2056].rearrange("p (g n) -> p g n", g=8)
        scT = work[:, 2064:3088].rearrange("p (t h n) -> p t h n", t=NT, h=4)
        otmp = work[:, 0:1024].rearrange("p (h n) -> p h n", h=4)
        latf = lat[:, :, :].rearrange("p a b -> p (a b)")
        hh = latf[:, 0:1024].rearrange("p (g n) -> p g n", g=8)
        latTf = latT[:, :, :].rearrange("p a b -> p (a b)")
        state = latTf[:, 0:516].rearrange("p (h n) -> p h n", h=4)
        kw = latTf[:, 520:1032].rearrange("p (h n) -> p h n", h=4)
        ktok = xmT[:, :, :].rearrange("p a b -> p (a b)")[:, 0:512].rearrange("p (h n) -> p h n", h=4)
        qiT, kiT = ogT, krT
        kk2 = qrT
        rel = xcT[:, :, :].rearrange("p (a b) n -> p a b n", a=2)
        score = vaug[:, :, :, :].rearrange("p a b c -> p (a b c)")[:, 0:512].rearrange("p (t n) -> p t n", t=NT)
        dmask = xmT[:, :, :].rearrange("p a b -> p (a b)")[:, 0:512].rearrange("p (t n) -> p t n", t=NT)

        chunks = weight_chunks(A)
        C = {c[0]: n for n, c in enumerate(chunks)}
        n_split, n_down, seen_s, seen_d = [], [], 0, 0
        for _, _, split, down in chunks:
            seen_s, seen_d = seen_s + split, seen_d + down
            n_split.append(seen_s)
            n_down.append(seen_d)
        tickets = bank_uses()
        T = {name: n for n, name in enumerate(tickets)}
        assert len(T) == len(tickets)
        norm_no = {n: i for i, n in enumerate(NORMS)}

        raw_full = [sem(f"raw_full{i}") for i in range(RING)]
        split_hi = sem("split_hi")
        split_lo = sem("split_lo")
        down_done = sem("down_done")
        bank_full = [sem(f"bank_full{i}") for i in range(BANKS)]
        bank_read = [sem(f"bank_read{i}") for i in range(BANKS)]
        silu_done, gu_done = sem("silu_done"), sem("gu_done")
        g_hi_done, g_lo_done = sem("g_hi_done"), sem("g_lo_done")
        square_done, rstd_done = sem("square_done"), sem("rstd_done")
        xn_done = sem("xn_done")
        h_hi_done = sem("h_hi_done")
        x_done = sem("x_done")
        gain_full = sem("gain_full")
        mem_split = sem("mem_split")
        mem_hi_done = sem("mem_hi_done")
        max_done, exp_done, prob_done = sem("max_done"), sem("exp_done"), sem("prob_done")
        o_hi_done = sem("o_hi_done")
        x_load, mem_load = sem("x_load"), sem("mem_load")
        gain_load, par_load = sem("gain_load"), sem("par_load")
        const_done, gates_load, pos_load = sem("const_done"), sem("gates_load"), sem("pos_load")
        sin_args, sin_done = sem("sin_args"), sem("sin_done")
        lat_done = sem("lat_done")
        rope_in, rope_done = sem("rope_in"), sem("rope_done")
        conv_done, silu_conv = sem("conv_done"), sem("silu_conv")
        skip_done = sem("skip_done")
        gate_abs, gate_exp, lf_done = sem("gate_abs"), sem("gate_exp"), sem("lf_done")
        diag_done, dm_done, decay_done = sem("diag_done"), sem("dm_done"), sem("decay_done")
        ex_in, ex_done = sem("ex_in"), sem("ex_done")
        kw_done, sc_done = sem("kw_done"), sem("sc_done")
        qc_scaled = sem("qc_scaled")
        var_done, vrstd_done, hn_done = sem("var_done"), sem("vrstd_done"), sem("hn_done")
        out_f, out_hi = sem("out_f"), sem("out_hi")
        ki_done, rel_done, rel_used = sem("ki_done"), sem("rel_done"), sem("rel_used")
        act_chain, dve_chain, pool_chain = sem("act_chain"), sem("dve_chain"), sem("pool_chain")
        out_done = sem("out_done")

        freed, count = {}, [0] * BANKS
        for n, name in enumerate(tickets):
            b = n % BANKS
            if name[0] in "GU":
                s, p = map(int, name[1:].split("."))
                v = FFNS[s] * PAIRS + p + 1
                freed[name] = (silu_done if name[0] == "G" else gu_done, v)
            else:
                count[b] += 1
                freed[name] = (bank_read[b], count[b])

        def full(name):
            n = T[name]
            return bank_full[n % BANKS], n // BANKS + 1

        def used(c):
            name, _, _, down = chunks[c]
            if down:
                return down_done, n_down[c]
            return full(LAST_USE.get(name, name))

        def bank(name):
            return psum[:, 4 + T[name] % BANKS, :]

        def gain(s, k):
            c = (s // 4 * 8 + 2 * (s % 4)) * KT + k
            return gcol[:, c:c + 1]

        CW, CB, GN, SK, CQ, CKV, CCQ, CCKV, MG = 0, 16, 20, 24, 28, 31, 33, 36, 38
        NP = MG + L * KT

        def later(pair, step, i):
            return pair[0], pair[1] + step * i

        block = ctx.enter_context(nc.Block())

        @block.sync
        def _(sp):
            sp.dma_start(x[:, :, :], A['x'][0].rearrange("(t p) n -> p t n", p=P)).then_inc(x_load, 16)
            sp.dma_start(grow[:, :], A['norm_g'].rearrange("l j (k p) -> (l j k) p", p=P)).then_inc(gain_load, 16)

            def slot_free(c, i=0):
                if c < RING:
                    return
                if chunks[c - RING][2]:
                    sp.wait_ge(split_lo, n_split[c - RING] + 6 * i)
                else:
                    sp.wait_ge(*used(c - RING))

            def load(c, src=None, i=0):
                slot_free(c, i)
                src = chunks[c][1] if src is None else src
                k, n = src.shape[1], src.shape[2]
                dst = raw[:, c % RING, 0:k * n].rearrange("p (k n) -> p k n", k=k)
                sp.dma_start(dst, src).then_inc(raw_full[c % RING], 16)

            def load_ffn(s):
                l, j = s // 4, (s % 4) // 2
                g, u, d = A['ffn_w_gate'][l, j], A['ffn_w_up'][l, j], A['ffn_w_down'][l, j]
                c0 = C[f"G{s}.0"]
                for c in range(c0, c0 + 8):
                    load(c)
                with sp.Fori(0, (PAIRS - 3) // 2) as i:
                    for q in range(2):
                        c = c0 + 8 + 3 * q
                        up = [w[:, bass.ds(i * (4 * P) + 2 * P * (3 + q), 2 * P)].rearrange("(k p) n -> p k n", p=P)
                              for w in (g, u)]
                        load(c, up[0], i)
                        load(c + 1, up[1], i)
                        load(c + 2, d[bass.ds(i * (4 * P) + 2 * P * (2 + q), 2 * P), :]
                             .rearrange("(k p) n -> p k n", p=P), i)
                load(C[f"D{s}.{PAIRS - 1}"])

            c = 0
            while c < len(chunks):
                if chunks[c][0][0] == "G":
                    load_ffn(int(chunks[c][0][1:].split(".")[0]))
                    c += 3 * PAIRS
                else:
                    load(c)
                    c += 1
            sp.wait_ge(x_done, SUBS)
            sp.dma_start(out[0].rearrange("(t p) n -> p t n", p=P), x[:, :, :]).then_inc(out_done, 16)
            sp.wait_ge(out_done, 16)

        @block.gpsimd
        def _(pool):
            done = [0]

            def link(ins):
                done[0] += 1
                ins.then_inc(pool_chain, 1)
                pool.wait_ge(pool_chain, done[0])

            pool.dma_start(stage, A['mem'][0].rearrange("(t p) n -> p t n", p=P)).then_inc(mem_load, 16)
            r = 0
            for name in ('ml_conv_w', 'ml_conv_b', 'ml_gn_g', 'ml_skip', 'mla_cq_g', 'mla_ckv_g', 'c_cq_g',
                         'c_ckv_g', 'mem_norm_g'):
                a = A[name]
                src = (a.rearrange("a j (k p) -> (a j k) p", p=P) if len(a.shape) == 3
                       else a.rearrange("a (k p) -> (a k) p", p=P))
                pool.dma_start(prow[r:r + src.shape[0], :], src).then_inc(par_load, 16)
                r += src.shape[0]
            assert r == NP
            with nc.allow_non_contiguous_dma(reason="256 positions, 96 gate rows"):
                pool.dma_start(pos_i[:, :], A['positions'].rearrange("a (t p) -> p (a t)", p=P)).then_inc(pos_load, 16)
                pool.dma_start(w_gates[:, :, :], A['ml_w_gates'][0].rearrange("(k p) n -> p k n", p=P))\
                    .then_inc(gates_load, 16)
            pool.dma_start(b_gates[:, :], A['ml_b_gates'].to_broadcast([P, 8])).then_inc(gates_load, 16)

            def load_gain(s):
                row = A['norm_g'][s // 4, 2 * (s % 4) + 1:2 * (s % 4) + 2, :]
                pool.dma_start(gain_row[:, :], row.to_broadcast([P, D])).then_inc(gain_full, 16)
            load_gain(0)

            link(pool.memset(ident[:, :], 0.0))
            link(pool.affine_select(out=ident[:, :], in_=ident[:, :], compare_op=ALU.not_equal, fill=1.0, base=0,
                                    pattern=[[-1, P]], channel_multiplier=1))
            pool.memset(minus_half[:, :], -0.5).then_inc(const_done, 1)
            for j in range(HALF):
                v = float(np.float32(10000.0 ** (-j / HALF)))
                ins = pool.memset(inv_freq[:, j:j + 1], v)
            ins.then_inc(const_done, 1)

            def rms(name):
                n = norm_no[name]
                pool.wait_ge(square_done, n + 1)
                link(pool.tensor_scalar(ms[:, n, :], ss[:, n, :], 1.0 / NORM_WIDTH.get(name, D), EPS,
                                        ALU.mult, ALU.add))
                pool.tensor_tensor(rstd[:, n, :], ms[:, n, :], minus_half[:, 0:NT], ALU.pow).then_inc(rstd_done, 1)

            rms("m")
            rms("pre0")
            link(pool.memset(ones[:, :], 1.0))
            link(pool.memset(cmask[:, :, :], 0.0))
            pool.affine_select(out=upper[:, :], in_=ones[:, :], compare_op=ALU.is_ge, fill=0.0, base=0,
                               pattern=[[1, P]], channel_multiplier=-1)
            for t in range(NT):
                pool.affine_select(out=cmask[:, t, :], in_=cmask[:, t, :], compare_op=ALU.is_ge, fill=NEG,
                                   base=P * t, pattern=[[-1, TOK]], channel_multiplier=1)
            pool.memset(xmT[:, :, 0:3], 0.0)
            pool.memset(vaug[:, :, :, HD:HD + 1], 1.0).then_inc(const_done, 1)

            for name in NORMS[2:]:
                if name == "post1":
                    pool.wait_ge(var_done, 1)
                    pool.tensor_tensor(small[:, 15, :], small[:, 14, :], minus_half[:, :], ALU.pow)\
                        .then_inc(vrstd_done, 1)
                rms(name)
                if name.startswith("post") and name != f"post{SUBS - 1}":
                    s = int(name[4:]) + 1
                    pool.wait_ge(x_done, s)
                    load_gain(s)

        @block.tensor
        def _(pe):
            order = iter(tickets)

            def take(name, i=0):
                n = T[name]
                if isinstance(i, int):
                    assert next(order) == name, name
                if n >= BANKS:
                    s, v = freed[tickets[n - BANKS]]
                    pe.wait_ge(s, v + (i * (1 if s not in (silu_done, gu_done) else 2)))
                return psum[:, 4 + n % BANKS, :]

            def filled(name, ins):
                ins.then_inc(bank_full[T[name] % BANKS], 1)

            def ready(name):
                pe.wait_ge(*freed[name])

            def weights(c, i=0):
                k, n = chunks[c][1].shape[1], chunks[c][1].shape[2]
                if chunks[c][2]:
                    pe.wait_ge(split_lo, n_split[c] + 6 * i)
                    return [w[:, c % RING, 0:k * n].rearrange("p (k n) -> p k n", k=k) for w in (w_hi, w_lo)]
                pe.wait_ge(raw_full[c % RING], 16 * (c // RING + 1))
                return raw[:, c % RING, 0:k * n].rearrange("p (k n) -> p k n", k=k)

            def feature_major(name, a_hi, a_lo, pairs=None, i=0):
                hi, lo = weights(C[name], i)
                out_ = take(name, i)
                for j in range(2):
                    o = out_[:, TOK * j:TOK * (j + 1)]
                    for k in range(KT):
                        if pairs and j == 0 and k % 2 == 0:
                            ready(f"h{pairs}.{k // 2}")
                        wh, wl = hi[:, k, P * j:P * (j + 1)], lo[:, k, P * j:P * (j + 1)]
                        nc.tensor.matmul(o, wh, a_hi[:, k, :], start=(k == 0), stop=False)
                        nc.tensor.matmul(o, wh, a_lo[:, k, :], start=False, stop=False)
                        last = nc.tensor.matmul(o, wl, a_hi[:, k, :], start=False, stop=(k == KT - 1))
                filled(name, last)

            def token_major(name, a_hi, a_lo, pairs=None):
                hi, lo = weights(C[name])
                n = chunks[C[name]][1].shape[2]
                out_ = take(name)
                for t in range(NT):
                    o = out_[:, 256 * t:256 * t + n]
                    for k in range(KT):
                        if pairs and t == 0 and k % 2 == 0:
                            ready(f"h{pairs}.{k // 2}")
                        ah, al = a_hi[:, k, P * t:P * (t + 1)], a_lo[:, k, P * t:P * (t + 1)]
                        nc.tensor.matmul(o, ah, hi[:, k, :], start=(k == 0), stop=False)
                        nc.tensor.matmul(o, ah, lo[:, k, :], start=False, stop=False)
                        last = nc.tensor.matmul(o, al, hi[:, k, :], start=False, stop=(k == KT - 1))
                filled(name, last)

            def down(c, a_hi, a_lo, first, final, i=0):
                hi, lo = weights(c, i)
                for k in range(2):
                    for t in range(NT):
                        ah, al = a_hi[:, k, P * t:P * (t + 1)], a_lo[:, k, P * t:P * (t + 1)]
                        for a, w in ((ah, hi), (ah, lo), (al, hi)):
                            for half in range(2):
                                last = nc.tensor.matmul(
                                    psum[:, 2 * t + half, :], a, w[:, k, 512 * half:512 * (half + 1)],
                                    start=(first and k == 0 and a is ah and w is hi),
                                    stop=(final and k == 1 and a is al))
                last.then_inc(down_done, 1)

            def transposes(name, tiles):
                out_ = take(name)
                for n, tile in enumerate(tiles):
                    last = nc.tensor.transpose(out_[:, P * n:P * (n + 1)], tile, ident[:, :])
                filled(name, last)

            def input_transposes(n, src):
                pe.wait_ge(xn_done, 1 if n == "m" else n + 2)
                for k in range(KT // 2):
                    transposes(f"h{n}.{k}", [src[:, t, P * kk:P * (kk + 1)] for kk in (2 * k, 2 * k + 1)
                                             for t in range(NT)])

            def ffn(s):
                base = FFNS[s] * PAIRS

                def act_ready(p, i=0):
                    pe.wait_ge(g_lo_done, base + p + 1 + 2 * i)

                def triple(p, i=0, pairs=None):
                    feature_major(f"G{s}.{p + 1}", h_hi, h_lo, i=i)
                    feature_major(f"U{s}.{p + 1}", h_hi, h_lo, i=i)
                    act_ready(p, i)
                    down(C[f"D{s}.{p}"], g_hi[:, p % 2], g_lo[:, p % 2], p == 0, False, i)

                feature_major(f"G{s}.0", h_hi, h_lo, pairs=str(s))
                feature_major(f"U{s}.0", h_hi, h_lo)
                if s:
                    pe.wait_ge(x_done, s)
                triple(0)
                triple(1)
                with pe.Fori(0, (PAIRS - 3) // 2) as i:
                    triple(2, i)
                    triple(3, i)
                for name in skipped(s):
                    assert next(order) == name
                p = PAIRS - 1
                act_ready(p)
                down(C[f"D{s}.{p}"], g_hi[:, p % 2], g_lo[:, p % 2], False, True)

            def skipped(s):
                return [f"{w}{s}.{p}" for p in range(3, PAIRS) for w in "GU"]

            def down_rows(name, n, s):
                pe.wait_ge(x_done, s)
                for i in range(n):
                    down(C[f"{name}.{i}"], h_hi[:, 2 * i:2 * i + 2], h_lo[:, 2 * i:2 * i + 2], i == 0, i == n - 1)

            def scores(u):
                kind, t, pair = UNITS[u]
                name = f"score{u}"
                out_ = take(name)
                keys = XK if kind[:2] == "xa" else KTs
                for j in range(2):
                    h = 2 * pair + j
                    o = out_[:, TOK * j:TOK * (j + 1)]
                    rot = kind == "mla"
                    last = nc.tensor.matmul(o, QT[:, h, P * t:P * (t + 1)], keys[:, h, :], start=True, stop=not rot)
                    if rot:
                        last = nc.tensor.matmul(o, qrT[:, pair, P * t:P * (t + 1)], krT[:, j, :],
                                                start=False, stop=True)
                filled(name, last)

            def prob_transposes(u):
                pe.wait_ge(prob_done, u + 1)
                transposes(f"pT{u}", [p_sb[:, u % 2, j, P * k:P * (k + 1)] for j in range(2) for k in range(NT)])

            def values(u):
                kind, t, pair = UNITS[u]
                ready(f"pT{u}")
                out_ = take(f"pv{u}")
                for j in range(2):
                    h = 2 * pair + j
                    for k in range(NT):
                        v = (XV[:, k, HD * h:HD * (h + 1)] if kind[:2] == "xa"
                             else V[:, h // 4, k, HD * (h % 4):HD * (h % 4 + 1)])
                        last = nc.tensor.matmul(out_[:, P * j:P * (j + 1)], v, pT[:, u % 2, j, k, :],
                                                start=(k == 0), stop=(k == NT - 1))
                filled(f"pv{u}", last)

            def fill(name):
                if name[:2] == "xk":
                    feature_major(name, m_hi, m_lo)
                elif name[:2] == "xv":
                    token_major(name, m_hi, m_lo)
                else:
                    feature_major(name, h_hi, h_lo)

            def attention(key, fillers=()):
                us = units_of(key)
                scores(us[0])
                for n, u in enumerate(us):
                    if n + 1 < len(us):
                        scores(us[n + 1])
                    if n:
                        values(us[n - 1])
                    if n < len(fillers):
                        if fillers[n][:3] in ("xk0", "xk1") and fillers[n][-1] == "0":
                            pe.wait_ge(mem_split, int(fillers[n][2]) + 1)
                        fill(fillers[n])
                    prob_transposes(u)
                values(us[-1])

            def up(name, c, tiles):
                out_ = take(name)
                for cols, terms in tiles:
                    for n, (a, b) in enumerate(terms):
                        last = nc.tensor.matmul(out_[:, cols], a, b, start=(n == 0), stop=(n == len(terms) - 1))
                filled(name, last)

            def cross(l, s):
                input_transposes(s, xn)
                feature_major(f"xq{l}.0", h_hi, h_lo, pairs=str(s))
                feature_major(f"xq{l}.1", h_hi, h_lo)
                ready(f"xq{l}.0")
                ready(f"xq{l}.1")
                attention(f"xa{l}")
                ready(f"pv{units_of(f'xa{l}')[-1]}")
                down_rows(f"xo{l}", 2, s)

            def tile(a, t):
                return a[:, P * t:P * (t + 1)]

            pe.wait_ge(const_done, 1)
            pe.wait_ge(gain_load, 16)
            pe.wait_ge(par_load, 16 * 9)
            out_ = take("gains")
            nc.tensor.transpose(out_[:, 0:P], grow[:, :], ident[:, :])
            filled("gains", nc.tensor.transpose(out_[:, P:P + NP], prow[0:NP, :], ident[0:NP, 0:NP]))
            input_transposes("m", stage)
            input_transposes(0, xn)
            ffn(0)

            input_transposes(1, xn)
            for n, (name, _, _) in enumerate(AB_COLS[:8]):
                if name[:2] in ("ab", "vm"):
                    token_major(name, h_hi, h_lo, pairs="1" if n == 0 else None)
                else:
                    feature_major(name, h_hi, h_lo)
            pe.wait_ge(lat_done, 1)
            transposes("cqT.0", [lat[:, t, P * k:P * (k + 1)] for k in (0, 1) for t in range(NT)])
            transposes("cqT.1", [lat[:, t, P * 2:P * 3] for t in range(NT)])
            pe.wait_ge(lat_done, 2)
            transposes("ckvT", [lat[:, t, QL + P * k:QL + P * (k + 1)] for k in (0, 1) for t in range(NT)])
            ready("cqT.0")
            ready("cqT.1")
            for i in range(2):
                w = weights(C[f"uq.{i}"])
                hw = HD + ROPE
                up(f"uqn.{i}", None, [(slice(TOK * j, TOK * (j + 1)),
                                       [(w[:, k, hw * j:hw * j + HD], latT[:, k, :]) for k in range(3)])
                                      for j in range(2)])
                rope_w = w.rearrange("p k (j n) -> p k j n", j=2)[:, :, :, HD:hw]
                up(f"uqr.{i}", None, [(slice(P * t, P * (t + 1)),
                                       [(tile(latT[:, k, :], t), rope_w[:, k]) for k in range(3)])
                                      for t in range(NT)])
            ready("ckvT")
            w = weights(C["ukv"])
            for i in range(2):
                up(f"kT.{i}", None, [(slice(TOK * j, TOK * (j + 1)),
                                      [(w[:, k, 2 * HD * (2 * i + j):2 * HD * (2 * i + j) + HD], latT[:, 3 + k, :])
                                       for k in range(2)]) for j in range(2)])
            v_w = w.rearrange("p k (h n) -> p k h n", h=4)[:, :, :, HD:2 * HD]
            for t in range(NT):
                up(f"v.{t}", None, [(slice(0, 512), [(tile(latT[:, 3 + k, :], t), v_w[:, k]) for k in range(2)])])
            ready("vm.0")
            ready("vm.1")
            for i in range(2):
                transposes(f"vmT.{i}", [vaug[:, t, 2 * i + j, 0:HD] for j in range(2) for t in range(NT)])
            pe.wait_ge(rope_done, 1)
            for i in range(2):
                transposes(f"rT.{i}", [rout[:, t, 2 * (2 * i + j):2 * (2 * i + j) + 2, :]
                                       .rearrange("p a b -> p (a b)") for j in range(2) for t in range(NT)])
            for name in ("uqn.0", "uqn.1", "kT.0", "kT.1", "v.0", "v.1", "rT.0", "rT.1"):
                ready(name)
            attention("mla", FILL["mla"])

            w = weights(C["mwq"])
            pe.wait_ge(silu_conv, 1)
            for i in range(2):
                up(f"mq.{i}", None, [(slice(TOK * j, TOK * (j + 1)), [(w[:, 2 * i + j, :], xcT[:, 2 * i + j, :])])
                                     for j in range(2)])
            w = weights(C["mwk"])
            for i in range(2):
                up(f"mk.{i}", None, [(slice(TOK * j, TOK * (j + 1)), [(w[:, 2 * i + j, :], xcT[:, 2 * i + j, :])])
                                     for j in range(2)])
            up("ktok", None, [(slice(HD * h, HD * (h + 1)), [(xcT[:, h, 0:P], w[:, h, :])]) for h in range(4)])
            for name in ("mq.0", "mq.1", "mk.0", "mk.1", "vmT.0", "vmT.1"):
                ready(name)
            pe.wait_ge(gates_load, 32)
            feats = [a[:, h, :] for a in (mqT, mkT, vmT) for h in range(4)]
            up("gates", None, [(slice(8 * t, 8 * t + 8), [(tile(f, t), w_gates[:, k, :]) for k, f in enumerate(feats)])
                               for t in range(NT)])
            token_major("xv0.1", m_hi, m_lo)
            pe.wait_ge(lf_done, 1)
            lf = small[:, 2:4, 0:4]
            up("cum", None, [(slice(0, 4), [(upper[:, :], lf[:, 0, :])]), (slice(4, 8), [(upper[:, :], lf[:, 1, :])]),
                             (slice(8, 12), [(ones[:, :], lf[:, 0, :])])])
            for t in range(NT):
                pe.wait_ge(diag_done, t + 1)
                up(f"arow.{t}", None, [(slice(0, 512), [(ones[:, :], dga[:, t].rearrange("p h n -> p (h n)"))])])
            for t in range(NT):
                up(f"S.{t}", None, [(slice(P * h, P * (h + 1)), [(tile(mqT[:, h, :], t), tile(mkT[:, h, :], t))])
                                    for h in range(4)])
            pe.wait_ge(kw_done, 1)
            for i in range(2):
                up(f"state.{i}", None, [(slice(256 * j, 256 * j + HD + 1),
                                         [(kw[:, 2 * i + j, :], vaug[:, 0, 2 * i + j, :])]) for j in range(2)])
            for t in range(NT):
                pe.wait_ge(sc_done, t + 1)
                transposes(f"scT.{t}", [sc[:, t, h, :] for h in range(4)])
            ready("state.0")
            ready("state.1")
            for i in range(2):
                up(f"qc.{i}", None, [(slice(256 * j, 256 * j + HD + 1),
                                      [(mqT[:, 2 * i + j, P:2 * P], state[:, 2 * i + j, :])]) for j in range(2)])
            for t in range(NT):
                ready(f"scT.{t}")
                for i in range(2):
                    up(f"num{t}.{i}", None, [(slice(256 * j, 256 * j + HD + 1),
                                              [(scT[:, t, 2 * i + j, :], vaug[:, t, 2 * i + j, :])])
                                             for j in range(2)])
            pe.wait_ge(hn_done, 1)
            for i in range(2):
                transposes(f"hnT.{i}", [hh[:, 4 * t + 2 * i + j, :] for j in range(2) for t in range(NT)])
            ready(f"pv{units_of('mla')[-1]}")
            pe.wait_ge(out_f, 4)
            down_rows("abo", 4, 1)
            cross(0, 2)
            for s in (3, 4):
                input_transposes(s, xn)
                ffn(s)

            input_transposes(5, xn)
            for n, (name, _, _) in enumerate(C_COLS):
                if name[:2] == "qi":
                    feature_major(name, h_hi, h_lo)
                else:
                    token_major(name, h_hi, h_lo, pairs="5" if n == 0 else None)
            pe.wait_ge(lat_done, 3)
            transposes("ccqT.0", [lat[:, t, P * k:P * (k + 1)] for k in (0, 1) for t in range(NT)])
            transposes("ccqT.1", [lat[:, t, P * 2:P * 3] for t in range(NT)])
            pe.wait_ge(lat_done, 4)
            transposes("cckvT", [lat[:, t, QL + P * k:QL + P * (k + 1)] for k in (0, 1) for t in range(NT)])
            pe.wait_ge(ki_done, 1)
            transposes("kiT", [kk2[:, t, P * j:P * (j + 1)] for j in range(2) for t in range(NT)])
            ready("qi.0")
            ready("qi.1")
            ready("kiT")
            for t in range(NT):
                for i in range(4):
                    up(f"rel{t}.{i}", None, [(slice(TOK * j, TOK * (j + 1)),
                                              [(qiT[:, i, P * t:P * (t + 1)], kiT[:, j, :])])
                                             for j in range(2)])
            ready("ccqT.0")
            ready("ccqT.1")
            for i in range(2):
                w = weights(C[f"cuq.{i}"])
                for m in range(2):
                    up(f"cuq.{i}.{m}", None, [(slice(TOK * j, TOK * (j + 1)),
                                               [(w[:, k, HD * (2 * m + j):HD * (2 * m + j + 1)], latT[:, k, :])
                                                for k in range(3)]) for j in range(2)])
            ready("cckvT")
            for i in range(4):
                w = weights(C[f"cuk_{i // 2}"]).rearrange("p (h k) n -> p h k n", h=4)
                up(f"cuk.{i}", None, [(slice(TOK * j, TOK * (j + 1)),
                                       [(w[:, 2 * (i % 2) + j, k, :], latT[:, 3 + k, :]) for k in range(2)])
                                      for j in range(2)])
            for i in range(2):
                w = weights(C[f"cuv_{i}"]).rearrange("p (h k) n -> p h k n", h=4)
                for t in range(NT):
                    up(f"cuv.{i}.{t}", None, [(slice(0, 512), [(tile(latT[:, 3 + k, :], t), w[:, :, k, :])
                                                              for k in range(2)])])
            for name in ("cuq.0.0", "cuq.0.1", "cuq.1.0", "cuq.1.1", "cuk.0", "cuk.1", "cuk.2", "cuk.3",
                         "cuv.0.0", "cuv.0.1", "cuv.1.0", "cuv.1.1"):
                ready(name)
            attention("dsa", FILL["dsa"])
            ready(f"pv{units_of('dsa')[-1]}")
            down_rows("co", 4, 5)
            cross(1, 6)
            input_transposes(7, xn)
            ffn(7)
            assert next(order, None) is None

        @block.scalar
        def _(act):
            done = [0]
            nxt = [0]

            def link(ins):
                done[0] += 1
                ins.then_inc(act_chain, 1)
                act.wait_ge(act_chain, done[0])

            def hi_half(c, i=0):
                k, n = chunks[c][1].shape[1], chunks[c][1].shape[2]
                act.wait_ge(raw_full[c % RING], 16 * (c // RING + 1) + 32 * i)
                if c >= RING:
                    s, v = used(c - RING)
                    act.wait_ge(s, v + (2 if s is down_done else 1) * i)
                nc.scalar.activation(w_hi[:, c % RING, 0:k * n], raw[:, c % RING, 0:k * n], ACT.Copy)\
                    .then_inc(split_hi, 1)

            def split_to(c):
                while nxt[0] <= min(c, len(chunks) - 1):
                    if chunks[nxt[0]][2]:
                        hi_half(nxt[0])
                    nxt[0] += 1

            def evacuate(name, dst, src=None, func=ACT.Copy, scale=1.0):
                act.wait_ge(*full(name))
                nc.scalar.activation(dst, bank(name) if src is None else src, func, scale=scale)\
                    .then_inc(freed[name][0], 1)

            def squares(name, src):
                n = norm_no[name]
                w = src[0].shape[-1]
                if n:
                    act.wait_ge(square_done, n)
                for t in range(NT):
                    ins = nc.scalar.activation(junk[:, t, 0:w], src[t], ACT.Square, accum_out=ss[:, n, t:t + 1])
                ins.then_inc(square_done, 1)

            def pre_norm(s):
                act.wait_ge(x_done, s)
                squares(f"pre{s}", [x[:, t, :] for t in range(NT)])

            def input_hi(s):
                for k in range(KT // 2):
                    name = f"h{s}.{k}"
                    act.wait_ge(*full(name))
                    for j in range(2):
                        ins = nc.scalar.activation(h_hi[:, 2 * k + j, :], bank(name)[:, TOK * j:TOK * (j + 1)],
                                                   ACT.Copy, scale=gain(s, 2 * k + j))
                    ins.then_inc(h_hi_done, 1)

            def post_norm(s, last_chunk):
                act.wait_ge(down_done, n_down[last_chunk])
                squares(f"post{s}", [y[:, t, :] for t in range(NT)])

            def ffn(s):
                c0, base = C[f"G{s}.0"], FFNS[s] * PAIRS

                def silu(p, i=0):
                    act.wait_ge(*later(full(f"G{s}.{p}"), 1, i))
                    nc.scalar.activation(sg[:, p % 2, :], bank(f"G{s}.{p}"), ACT.Silu).then_inc(silu_done, 1)

                def act_hi(p, i=0):
                    act.wait_ge(gu_done, base + p + 1 + 2 * i)
                    nc.scalar.activation(g_hi[:, p % 2].rearrange("p a n -> p (a n)"), gu[:, p % 2, :], ACT.Copy)\
                        .then_inc(g_hi_done, 1)

                def triple(p, i=0):
                    c = c0 + 2 + 3 * p
                    hi_half(c, i)
                    silu(p, i)
                    hi_half(c + 1, i)
                    act_hi(p, i)
                    hi_half(c + 2, i)

                split_to(c0 + 1)
                triple(0)
                triple(1)
                with act.Fori(0, (PAIRS - 3) // 2) as i:
                    triple(2, i)
                    triple(3, i)
                nxt[0] = c0 + 3 * PAIRS - 1
                split_to(nxt[0])
                silu(PAIRS - 1)
                split_to(nxt[0])
                act_hi(PAIRS - 1)
                split_to(nxt[0])
                post_norm(s, C[f"D{s}.{PAIRS - 1}"])

            def mem_hi(l):
                for k in range(KT):
                    ins = nc.scalar.activation(m_hi[:, k, :], memT[:, k, :], ACT.Copy,
                                               scale=pcol[:, MG + l * KT + k:MG + l * KT + k + 1])
                ins.then_inc(mem_hi_done, 1)

            def exps(u):
                kind = UNITS[u][0]
                act.wait_ge(max_done, u + 1)
                xa = kind[:2] == "xa"
                for j in range(2):
                    src = bank(f"score{u}")[:, TOK * j:TOK * (j + 1)] if xa else s_sb[:, u % 2, j, :]
                    ins = nc.scalar.activation(p_sb[:, u % 2, j, :], src, ACT.Exp, bias=nmax[:, u, j:j + 1],
                                               scale=HD ** -0.5 if xa else 1.0, accum_out=esum[:, u, j:j + 1])
                ins.then_inc(exp_done, 1)

            def prob_copy(u):
                evacuate(f"pT{u}", pT[:, u % 2].rearrange("p h k n -> p (h k n)"))

            def output_hi(u):
                kind, t, pair = UNITS[u]
                act.wait_ge(*full(f"pv{u}"))
                nc.scalar.activation(h_hi[:, 2 * pair:2 * pair + 2, P * t:P * (t + 1)],
                                     bank(f"pv{u}")[:, 0:2 * P].rearrange("p (h n) -> p h n", h=2), ACT.Copy)\
                    .then_inc(o_hi_done, 1)

            def fill(name):
                split_to(C[name] + 2)
                i = int(name[-1])
                if name[:2] == "xk":
                    evacuate(name, XK[:, 2 * i:2 * i + 2, :].rearrange("p h n -> p (h n)"))
                elif name[:2] == "xv":
                    evacuate(name, XV[:, :, 256 * i:256 * (i + 1)], bank(name).rearrange("p (t n) -> p t n", t=NT))
                elif name[:2] == "og":
                    evacuate(name, ogT[:, 2 * i:2 * i + 2, :].rearrange("p h n -> p (h n)"), func=ACT.Sigmoid)

            def attention(key, fillers=()):
                us = units_of(key)
                for n, u in enumerate(us):
                    exps(u)
                    if n:
                        output_hi(us[n - 1])
                    if n < len(fillers):
                        fill(fillers[n])
                    prob_copy(u)
                output_hi(us[-1])

            def latents(names, norms):
                for i, (name, c0, c1) in enumerate(names):
                    split_to(C[name] + 2)
                    c1 = min(c1, QL + KVL)
                    evacuate(name, lat[:, :, c0:c1],
                             bank(name).rearrange("p (t n) -> p t n", t=NT)[:, :, 0:c1 - c0])

            def cross(l, s):
                pre_norm(s)
                input_hi(s)
                for i in range(2):
                    split_to(C[f"xq{l}.{i}"] + 2)
                    evacuate(f"xq{l}.{i}", QT[:, 2 * i:2 * i + 2, :].rearrange("p h n -> p (h n)"))
                attention(f"xa{l}")
                for i in range(2):
                    split_to(C[f"xo{l}.{i}"] + 2)
                post_norm(s, C[f"xo{l}.1"])

            split_to(1)
            act.wait_ge(mem_load, 16)
            squares("m", [stage[:, t, :] for t in range(NT)])
            act.wait_ge(x_load, 16)
            squares("pre0", [x[:, t, :] for t in range(NT)])
            act.wait_ge(*full("gains"))
            link(nc.scalar.activation(gcol[:, :], bank("gains")[:, 0:P], ACT.Copy))
            evacuate("gains", pcol[:, 0:NP], bank("gains")[:, P:P + NP])
            act.wait_ge(*freed["gains"])
            for k in range(KT // 2):
                evacuate(f"hm.{k}", memT[:, 2 * k:2 * k + 2, :].rearrange("p a n -> p (a n)"))
            input_hi(0)
            act.wait_ge(sin_args, 1)
            nc.scalar.activation(ang[:, 2:4].rearrange("p a t n -> p (a t n)"),
                                 ang[:, 0:2].rearrange("p a t n -> p (a t n)"), ACT.Sin).then_inc(sin_done, 1)
            ffn(0)

            pre_norm(1)
            input_hi(1)
            for name, c0, c1 in AB_COLS[:3]:
                split_to(C[name] + 2)
                hi = min(c1, QL + KVL)
                src = bank(name).rearrange("p (t n) -> p t n", t=NT)
                act.wait_ge(*full(name))
                if c1 > hi:
                    nc.scalar.activation(rin[:, :, 4, :], src[:, :, hi - c0:c1 - c0], ACT.Copy)
                nc.scalar.activation(lat[:, :, c0:hi], src[:, :, 0:hi - c0], ACT.Copy).then_inc(freed[name][0], 1)
            act.wait_ge(*freed["ab.1"])
            squares("cq", [lat[:, t, 0:QL] for t in range(NT)])
            act.wait_ge(*freed["ab.2"])
            squares("ckv", [lat[:, t, QL:QL + KVL] for t in range(NT)])
            mem_hi(0)
            for i in range(2):
                split_to(C[f"xm.{i}"] + 2)
                evacuate(f"xm.{i}", xmT[:, 2 * i:2 * i + 2, 3:3 + TOK],
                         bank(f"xm.{i}").rearrange("p (h n) -> p h n", h=2))
            for i in range(2):
                split_to(C[f"vm.{i}"] + 2)
                evacuate(f"vm.{i}", vaug[:, :, 2 * i:2 * i + 2, 0:HD],
                         bank(f"vm.{i}").rearrange("p (t h n) -> p t h n", t=NT, h=2))
            act.wait_ge(conv_done, 1)
            nc.scalar.activation(xcT[:, :, :].rearrange("p h n -> p (h n)"), ogT[:, :, :].rearrange("p h n -> p (h n)"),
                                 ACT.Silu).then_inc(silu_conv, 1)
            act.wait_ge(silu_conv, 1)
            fill("og.0")
            for name, k in (("cqT.0", 0), ("cqT.1", 2), ("ckvT", 3)):
                n = 1 if name == "cqT.1" else 2
                act.wait_ge(*full(name))
                for j in range(n):
                    ins = nc.scalar.activation(latT[:, k + j, :], bank(name)[:, TOK * j:TOK * (j + 1)], ACT.Copy,
                                               scale=pcol[:, CQ + k + j:CQ + k + j + 1])
                ins.then_inc(freed[name][0], 1)
            for i in range(2):
                evacuate(f"uqn.{i}", QT[:, 2 * i:2 * i + 2, :].rearrange("p h n -> p (h n)"))
                act.wait_ge(*full(f"uqr.{i}"))
                for t in range(NT):
                    ins = nc.scalar.activation(rin[:, t, 2 * i:2 * i + 2, :], bank(f"uqr.{i}")[:, P * t:P * (t + 1)]
                                               .rearrange("p (h n) -> p h n", h=2), ACT.Copy)
                ins.then_inc(freed[f"uqr.{i}"][0], 1)
            for i in range(2):
                evacuate(f"kT.{i}", KTs[:, 2 * i:2 * i + 2, :].rearrange("p h n -> p (h n)"))
            for t in range(NT):
                evacuate(f"v.{t}", V[:, 0, t, :])
            for i in range(2):
                evacuate(f"vmT.{i}", vmT[:, 2 * i:2 * i + 2, :].rearrange("p h n -> p (h n)"))
            evacuate("rT.0", qrT[:, :, :].rearrange("p h n -> p (h n)"))
            evacuate("rT.1", krT[:, :, :].rearrange("p h n -> p (h n)"))
            attention("mla", FILL["mla"])
            for n, dst in (("mq", mqT), ("mk", mkT)):
                for i in range(2):
                    evacuate(f"{n}.{i}", dst[:, 2 * i:2 * i + 2, :].rearrange("p h n -> p (h n)"))
            evacuate("ktok", ktok.rearrange("p h n -> p (h n)"))
            act.wait_ge(gate_abs, 1)
            link(nc.scalar.activation(small[:, 4:6, 0:4], small[:, 4:6, 0:4], ACT.Exp, scale=-1.0))
            nc.scalar.activation(small[:, 6:8, 0:4], small[:, 4:6, 0:4], ACT.Ln, bias=1.0).then_inc(gate_exp, 1)
            fill("xv0.1")
            act.wait_ge(ex_in, 1)
            nc.scalar.activation(small[:, 18:20, :], small[:, 16:18, :], ACT.Exp).then_inc(ex_done, 1)
            for t in range(NT):
                act.wait_ge(dm_done, t + 1)
                nc.scalar.activation(Dm[:, t].rearrange("p h n -> p (h n)"), Dm[:, t].rearrange("p h n -> p (h n)"),
                                     ACT.Exp).then_inc(decay_done, 1)
            for i in range(2):
                evacuate(f"state.{i}", state[:, 2 * i:2 * i + 2, :],
                         bank(f"state.{i}").rearrange("p (h n) -> p h n", h=2)[:, :, 0:HD + 1])
            for t in range(NT):
                evacuate(f"scT.{t}", scT[:, t].rearrange("p h n -> p (h n)"))
            for i in range(2):
                act.wait_ge(*full(f"qc.{i}"))
                for j in range(2):
                    h = 2 * i + j
                    ins = nc.scalar.activation(qcs[:, h, :], bank(f"qc.{i}")[:, 256 * j:256 * j + HD + 1], ACT.Copy,
                                               scale=small[:, 18, 4 + h:5 + h])
                ins.then_inc(freed[f"qc.{i}"][0], 1)
            for i in range(2):
                act.wait_ge(out_hi, i + 1)
                nc.scalar.activation(h_hi[:, 4 + 2 * i:6 + 2 * i, :], otmp[:, 2 * i:2 * i + 2, :], ACT.Copy)\
                    .then_inc(o_hi_done, 1)
            for i in range(4):
                split_to(C[f"abo.{i}"] + 2)
            post_norm(1, C["abo.3"])
            cross(0, 2)
            for s in (3, 4):
                pre_norm(s)
                input_hi(s)
                ffn(s)

            pre_norm(5)
            input_hi(5)
            latents(C_COLS[:3], None)
            act.wait_ge(*freed["c.1"])
            act.wait_ge(*freed["c.2"])
            squares("ccq", [lat[:, t, 0:QL] for t in range(NT)])
            squares("cckv", [lat[:, t, QL:QL + KVL] for t in range(NT)])
            mem_hi(1)
            for i in range(2):
                split_to(C[f"qi.{i}"] + 2)
                evacuate(f"qi.{i}", qiT[:, 2 * i:2 * i + 2, :].rearrange("p h n -> p (h n)"))
            for name, k in (("ccqT.0", 0), ("ccqT.1", 2), ("cckvT", 3)):
                n = 1 if name == "ccqT.1" else 2
                act.wait_ge(*full(name))
                for j in range(n):
                    ins = nc.scalar.activation(latT[:, k + j, :], bank(name)[:, TOK * j:TOK * (j + 1)], ACT.Copy,
                                               scale=pcol[:, CCQ + k + j:CCQ + k + j + 1])
                ins.then_inc(freed[name][0], 1)
            evacuate("kiT", kiT[:, :, :].rearrange("p h n -> p (h n)"))
            for n in range(8):
                t, i = divmod(n, 4)
                if n >= 2:
                    act.wait_ge(rel_used, n - 1)
                evacuate(f"rel{t}.{i}", rel[:, n % 2].rearrange("p h n -> p (h n)"), func=ACT.Relu)
            for i in range(2):
                for m in range(2):
                    evacuate(f"cuq.{i}.{m}", QT[:, 4 * i + 2 * m:4 * i + 2 * m + 2, :].rearrange("p h n -> p (h n)"))
            for i in range(4):
                evacuate(f"cuk.{i}", KTs[:, 2 * i:2 * i + 2, :].rearrange("p h n -> p (h n)"))
            split_to(C["xk1.0"])
            for i in range(2):
                for t in range(NT):
                    evacuate(f"cuv.{i}.{t}", V[:, i, t, :])
            attention("dsa", FILL["dsa"])
            for i in range(4):
                split_to(C[f"co.{i}"] + 2)
            post_norm(5, C["co.3"])
            cross(1, 6)
            pre_norm(7)
            input_hi(7)
            ffn(7)

        def mlstm(dve, link, split_to):
            def heads(a, n=HD):
                return a.unsqueeze(2).to_broadcast([P, 4, n])

            sm = small
            lf, ax_, e1, bc, a_ = sm[:, 2:4, 0:4], sm[:, 4:6, 0:4], sm[:, 6:8, 0:4], sm[:, 8:10, 0:4], sm[:, 10:12, 0:4]
            btot, mj = sm[:, 8, 4:8], sm[:, 12:14, 0:4]
            w0, mnew = sm[:, 12, 4:8], sm[:, 13, 4:8]
            dve.wait_ge(gates_load, 32)
            dve.wait_ge(*full("gates"))
            nc.vector.tensor_tensor(gts[:, :, :], bank("gates")[:, 0:16].rearrange("p (t n) -> p t n", t=NT),
                                    b_gates[:, :].unsqueeze(1).to_broadcast([P, NT, 8]), ALU.add)\
                .then_inc(freed["gates"][0], 1)
            dve.wait_ge(*freed["gates"])
            li, f = gts[:, :, 0:4], gts[:, :, 4:8]
            nc.vector.scalar_tensor_tensor(ax_, f, -1.0, f, ALU.mult, ALU.max).then_inc(gate_abs, 1)
            split_to(C["xv0.1"] + 2)
            dve.wait_ge(gate_exp, 1)
            nc.vector.scalar_tensor_tensor(lf, f, 0.0, e1, ALU.min, ALU.subtract).then_inc(lf_done, 1)
            dve.wait_ge(*full("cum"))
            b = bank("cum")
            nc.vector.tensor_copy(bc, b[:, 0:8].rearrange("p (t n) -> p t n", t=NT))
            nc.vector.tensor_copy(btot, b[:, 8:12]).then_inc(freed["cum"][0], 1)
            dve.wait_ge(*freed["cum"])
            link(nc.vector.tensor_tensor(a_, li, bc, ALU.subtract))
            for t in range(NT):
                nc.vector.tensor_tensor(dga[:, t], ident[:, :].unsqueeze(1).to_broadcast([P, 4, P]), heads(a_[:, t, :]),
                                        ALU.mult).then_inc(diag_done, 1)
            tri = cmask[:, 0, 0:P].unsqueeze(1).to_broadcast([P, 4, P])
            for t in range(NT):
                name = f"arow.{t}"
                dve.wait_ge(*full(name))
                row = bank(name).rearrange("p (h n) -> p h n", h=4)
                if t == 0:
                    link(nc.vector.tensor_reduce(w0, row, AX.X, ALU.max))
                nc.vector.tensor_tensor(Dm[:, t], row, tri, ALU.add).then_inc(freed[name][0], 1)
                dve.wait_ge(*freed[name])
                link(nc.vector.tensor_reduce(mj[:, t, :], Dm[:, t], AX.X, ALU.max))
                if t == 0:
                    link(nc.vector.tensor_scalar(w0, w0, 0.0, None, ALU.max))
                    link(nc.vector.tensor_tensor(mnew, btot, w0, ALU.add))
                    link(nc.vector.tensor_scalar(mj[:, 0, :], mj[:, 0, :], 0.0, None, ALU.max))
                else:
                    link(nc.vector.tensor_tensor(mj[:, 1, :], mj[:, 1, :], mnew, ALU.max))
                nc.vector.tensor_tensor(Dm[:, t], Dm[:, t], heads(mj[:, t, :]), ALU.subtract).then_inc(dm_done, 1)
            ex = sm[:, 16:18, :]
            nc.vector.tensor_tensor(ex[:, 0, 0:4], a_[:, 0, :], w0, ALU.subtract)
            nc.vector.tensor_tensor(ex[:, 0, 4:8], mnew, mj[:, 1, :], ALU.subtract)
            link(nc.vector.tensor_tensor(ex[:, 1, :].rearrange("p (t n) -> p t n", t=NT), bc, mj, ALU.add))
            nc.vector.tensor_scalar(ex[:, 1, :], ex[:, 1, :], -1.0, None, ALU.mult).then_inc(ex_in, 1)
            dve.wait_ge(ex_done, 1)
            dve.wait_ge(*freed["ktok"])
            nc.vector.scalar_tensor_tensor(kw, ktok, HD ** -0.5, heads(sm[:, 18, 0:4]), ALU.mult, ALU.mult)\
                .then_inc(kw_done, 1)
            for t in range(NT):
                name = f"S.{t}"
                dve.wait_ge(decay_done, t + 1)
                dve.wait_ge(*full(name))
                nc.vector.scalar_tensor_tensor(sc[:, t], bank(name).rearrange("p (h n) -> p h n", h=4), HD ** -0.5,
                                               Dm[:, t], ALU.mult, ALU.mult).then_inc(freed[name][0], 1)
                dve.wait_ge(*freed[name])
                nc.vector.tensor_copy(sm[:, 20, 0:1], sm[:, 18, 0:1]).then_inc(sc_done, 1)
            for t in range(NT):
                for i in range(2):
                    name = f"num{t}.{i}"
                    dve.wait_ge(*full(name))
                    src = bank(name).rearrange("p (h n) -> p h n", h=2)[:, :, 0:HD + 1]
                    dst = nd[:, t, 2 * i:2 * i + 2, :]
                    if t == 0:
                        nc.vector.tensor_copy(dst, src).then_inc(freed[name][0], 1)
                    else:
                        dve.wait_ge(*freed[f"qc.{i}"])
                        nc.vector.tensor_tensor(dst, src, qcs[:, 2 * i:2 * i + 2, :], ALU.add)\
                            .then_inc(freed[name][0], 1)
                    dve.wait_ge(*freed[name])
            den = sm[:, 14, :]
            en = sm[:, 19, :]
            ndg = nd.rearrange("p t h n -> p (t h) n")
            dsum = ndg[:, :, HD:HD + 1].rearrange("p g n -> p (g n)")
            link(nc.vector.scalar_tensor_tensor(den, dsum, -1.0, dsum, ALU.mult, ALU.max))
            link(nc.vector.tensor_tensor(den, den, en, ALU.max))
            link(nc.vector.reciprocal(den, den))

            def groups(a):
                return a.unsqueeze(2).to_broadcast([P, 8, HD])
            link(nc.vector.tensor_tensor(hh, ndg[:, :, 0:HD], groups(den), ALU.mult))
            mean = sm[:, 21, :]
            link(nc.vector.tensor_reduce(mean, hh, AX.X, ALU.add))
            link(nc.vector.tensor_scalar(mean, mean, 1.0 / HD, None, ALU.mult))
            link(nc.vector.tensor_tensor(hh, hh, groups(mean), ALU.subtract))
            link(nc.vector.tensor_tensor(sq, hh, hh, ALU.mult))
            link(nc.vector.tensor_reduce(sm[:, 22, :], sq, AX.X, ALU.add))
            nc.vector.tensor_scalar(sm[:, 14, :], sm[:, 22, :], 1.0 / HD, EPS, ALU.mult, ALU.add).then_inc(var_done, 1)
            for h in range(4):
                ins = nc.vector.tensor_scalar(xcT[:, h, :], xcT[:, h, :], pcol[:, SK + h:SK + h + 1], None, ALU.mult)
            link(ins)
            dve.wait_ge(vrstd_done, 1)
            nc.vector.tensor_tensor(hh, hh, groups(sm[:, 15, :]), ALU.mult).then_inc(hn_done, 1)
            for i in range(2):
                name = f"hnT.{i}"
                dve.wait_ge(*full(name))
                for j in range(2):
                    h = 2 * i + j
                    ins = nc.vector.scalar_tensor_tensor(otmp[:, h, :], bank(name)[:, TOK * j:TOK * (j + 1)],
                                                         pcol[:, GN + h:GN + h + 1], xcT[:, h, :], ALU.mult, ALU.add)
                ins.then_inc(freed[name][0], 1)
                dve.wait_ge(*freed[name])
                nc.vector.tensor_tensor(otmp[:, 2 * i:2 * i + 2, :], otmp[:, 2 * i:2 * i + 2, :],
                                        ogT[:, 2 * i:2 * i + 2, :], ALU.mult).then_inc(out_hi, 1)
                dve.wait_ge(out_hi, i + 1)
            for i in range(2):
                dve.wait_ge(o_hi_done, 4 + i + 1)
                for k in (4 + 2 * i, 5 + 2 * i):
                    nc.vector.tensor_tensor(h_lo[:, k, :], otmp[:, k - 4, :], h_hi[:, k, :].bitcast(F32),
                                            ALU.subtract).then_inc(out_f, 1)

        @block.vector
        def _(dve):
            done = [0]
            nxt = [0]
            outs = [0]

            def link(ins):
                done[0] += 1
                ins.then_inc(dve_chain, 1)
                dve.wait_ge(dve_chain, done[0])

            def lo_half(c, i=0):
                k, n = chunks[c][1].shape[1], chunks[c][1].shape[2]
                dve.wait_ge(split_hi, n_split[c] + 6 * i)
                nc.vector.tensor_tensor(w_lo[:, c % RING, 0:k * n], raw[:, c % RING, 0:k * n],
                                        w_hi[:, c % RING, 0:k * n].bitcast(F32), ALU.subtract).then_inc(split_lo, 1)

            def split_to(c):
                while nxt[0] <= min(c, len(chunks) - 1):
                    if chunks[nxt[0]][2]:
                        lo_half(nxt[0])
                    nxt[0] += 1

            def scale_rows(name, src, dst, w):
                n = norm_no[name]
                dve.wait_ge(rstd_done, n + 1)
                for t in range(NT):
                    ins = nc.vector.tensor_scalar(dst[:, t, :], src[:, t, :], rstd[:, n, t:t + 1], None, ALU.mult)
                return ins

            def input_lo(s):
                hs = [f"h{s}.{k}" for k in range(KT // 2)]
                first = hi_base[s]
                for k, name in enumerate(hs):
                    dve.wait_ge(h_hi_done, first + k + 1)
                    for j in range(2):
                        kk = 2 * k + j
                        ins = nc.vector.scalar_tensor_tensor(h_lo[:, kk, :], bank(name)[:, TOK * j:TOK * (j + 1)],
                                                             gain(s, kk), h_hi[:, kk, :].bitcast(F32),
                                                             ALU.mult, ALU.subtract)
                    ins.then_inc(freed[name][0], 1)

            hi_base = {s: 4 * s for s in range(SUBS)}

            def pre_norm(s):
                scale_rows(f"pre{s}", x, xn, D).then_inc(xn_done, 1)
                input_lo(s)

            def post_norm(s):
                n = norm_no[f"post{s}"]
                dve.wait_ge(rstd_done, n + 1)
                dve.wait_ge(gain_full, 16 * (s + 1))
                for t in range(NT):
                    link(nc.vector.scalar_tensor_tensor(stage[:, t, :], y[:, t, :], rstd[:, n, t:t + 1],
                                                        gain_row[:, :], ALU.mult, ALU.mult))
                for t in range(NT):
                    ins = nc.vector.scalar_tensor_tensor(x[:, t, :], stage[:, t, :], 0.5 if s in FFNS else 1.0,
                                                         x[:, t, :], ALU.mult, ALU.add)
                ins.then_inc(x_done, 1)

            def ffn(s):
                c0, base = C[f"G{s}.0"], FFNS[s] * PAIRS

                def gate_up(p, i=0):
                    dve.wait_ge(silu_done, base + p + 1 + 2 * i)
                    dve.wait_ge(*later(full(f"U{s}.{p}"), 1, i))
                    nc.vector.tensor_tensor(gu[:, p % 2, :], sg[:, p % 2, :], bank(f"U{s}.{p}"), ALU.mult)\
                        .then_inc(gu_done, 1)

                def act_lo(p, i=0):
                    dve.wait_ge(g_hi_done, base + p + 1 + 2 * i)
                    nc.vector.tensor_tensor(g_lo[:, p % 2].rearrange("p a n -> p (a n)"), gu[:, p % 2, :],
                                            g_hi[:, p % 2].rearrange("p a n -> p (a n)").bitcast(F32),
                                            ALU.subtract).then_inc(g_lo_done, 1)

                def triple(p, i=0):
                    c = c0 + 2 + 3 * p
                    lo_half(c, i)
                    gate_up(p, i)
                    lo_half(c + 1, i)
                    act_lo(p, i)
                    lo_half(c + 2, i)

                split_to(c0 + 1)
                triple(0)
                triple(1)
                with dve.Fori(0, (PAIRS - 3) // 2) as i:
                    triple(2, i)
                    triple(3, i)
                nxt[0] = c0 + 3 * PAIRS - 1
                split_to(nxt[0])
                gate_up(PAIRS - 1)
                split_to(nxt[0])
                act_lo(PAIRS - 1)
                split_to(nxt[0])
                post_norm(s)

            def mem_lo(l):
                dve.wait_ge(mem_hi_done, l + 1)
                for k in range(KT):
                    c = MG + l * KT + k
                    ins = nc.vector.scalar_tensor_tensor(m_lo[:, k, :], memT[:, k, :], pcol[:, c:c + 1],
                                                         m_hi[:, k, :].bitcast(F32), ALU.mult, ALU.subtract)
                ins.then_inc(mem_split, 1)

            def row_max(u):
                kind, t, pair = UNITS[u]
                name = f"score{u}"
                dve.wait_ge(*full(name))
                b = bank(name).rearrange("p (h n) -> p h n", h=2)
                if kind[:2] == "xa":
                    link(nc.vector.tensor_reduce(einv[:, u, :], b, AX.X, ALU.max))
                    nc.vector.tensor_scalar(nmax[:, u, :], einv[:, u, :], -HD ** -0.5, None, ALU.mult)\
                        .then_inc(max_done, 1)
                    return
                m = (cmask if kind == "mla" else dmask)[:, t, :].unsqueeze(1).to_broadcast([P, 2, TOK])
                scale = (HD + ROPE) ** -0.5 if kind == "mla" else HD ** -0.5
                nc.vector.scalar_tensor_tensor(s_sb[:, u % 2], b, scale, m, ALU.mult, ALU.add)\
                    .then_inc(freed[name][0], 1)
                dve.wait_ge(*freed[name])
                nc.vector.tensor_reduce(nmax[:, u, :], s_sb[:, u % 2], AX.X, ALU.max, negate=True)\
                    .then_inc(max_done, 1)

            def normalise(u):
                dve.wait_ge(exp_done, u + 1)
                ins = nc.vector.reciprocal(einv[:, u, :], esum[:, u, :])
                if UNITS[u][0][:2] == "xa":
                    ins.then_inc(freed[f"score{u}"][0], 1)
                    dve.wait_ge(*freed[f"score{u}"])
                else:
                    link(ins)
                nc.vector.tensor_tensor(p_sb[:, u % 2], p_sb[:, u % 2],
                                        einv[:, u, :].unsqueeze(2).to_broadcast([P, 2, TOK]), ALU.mult)\
                    .then_inc(prob_done, 1)

            def output_lo(u):
                kind, t, pair = UNITS[u]
                outs[0] += 1
                dve.wait_ge(o_hi_done, outs[0])
                o = (slice(None), slice(2 * pair, 2 * pair + 2), slice(P * t, P * (t + 1)))
                nc.vector.tensor_tensor(h_lo[o], bank(f"pv{u}")[:, 0:2 * P].rearrange("p (h n) -> p h n", h=2),
                                        h_hi[o].bitcast(F32), ALU.subtract).then_inc(freed[f"pv{u}"][0], 1)

            def attention(key, fillers=()):
                us = units_of(key)
                row_max(us[0])
                for n, u in enumerate(us):
                    if n + 1 < len(us):
                        row_max(us[n + 1])
                    normalise(u)
                    if n:
                        output_lo(us[n - 1])
                    if n < len(fillers):
                        split_to(C[fillers[n]] + 2)
                output_lo(us[-1])

            def cross(l, s):
                pre_norm(s)
                for i in range(2):
                    split_to(C[f"xq{l}.{i}"] + 2)
                attention(f"xa{l}")
                for i in range(2):
                    split_to(C[f"xo{l}.{i}"] + 2)
                post_norm(s)

            split_to(1)
            n = norm_no["m"]
            dve.wait_ge(rstd_done, 1)
            for t in range(NT):
                ins = nc.vector.tensor_scalar(stage[:, t, :], stage[:, t, :], rstd[:, n, t:t + 1], None, ALU.mult)
            ins.then_inc(xn_done, 1)
            dve.wait_ge(*freed["gains"])
            pre_norm(0)
            dve.wait_ge(pos_load, 16)
            dve.wait_ge(const_done, 2)
            link(nc.vector.tensor_copy(pos[:, :], pos_i[:, :]))
            for t in range(NT):
                ins = nc.vector.tensor_scalar(ang[:, 0, t, :], inv_freq[:, :], pos[:, t:t + 1], None, ALU.mult)
            link(ins)
            a0, a1, a2, a3 = (ang[:, i] for i in range(4))
            link(nc.vector.tensor_scalar(turns_i[:, :, :], a0, float(1 / (2 * np.pi)), None, ALU.mult))
            link(nc.vector.tensor_copy(a1, turns_i[:, :, :]))
            for part in TWO_PI:
                link(nc.vector.scalar_tensor_tensor(a0, a1, -part, a0, ALU.mult, ALU.add))
            link(nc.vector.tensor_scalar(a0, a0, 0.5, None, ALU.mult))
            link(nc.vector.scalar_tensor_tensor(a1, a0, -1.0, a0, ALU.mult, ALU.min))
            nc.vector.tensor_scalar(a1, a1, float(np.pi / 2), None, ALU.add).then_inc(sin_args, 1)
            dve.wait_ge(sin_done, 1)
            link(nc.vector.scalar_tensor_tensor(sin[:, :, :], a2, 2.0, a3, ALU.mult, ALU.mult))
            link(nc.vector.scalar_tensor_tensor(cos[:, :, :], a2, -2.0, a2, ALU.mult, ALU.mult))
            link(nc.vector.tensor_scalar(cos[:, :, :], cos[:, :, :], 1.0, None, ALU.add))
            ffn(0)

            pre_norm(1)
            for name, _, _ in AB_COLS[:3]:
                split_to(C[name] + 2)
            for name, a, b in (("cq", 0, QL), ("ckv", QL, QL + KVL)):
                scale_rows(name, lat[:, :, a:b], lat[:, :, a:b], b - a).then_inc(lat_done, 1)
            mem_lo(0)
            split_to(C["xm.0"] + 2)
            split_to(C["xm.1"] + 2)
            dve.wait_ge(const_done, 3)
            for i in range(2):
                dve.wait_ge(*freed[f"xm.{i}"])
                for h in (2 * i, 2 * i + 1):
                    link(nc.vector.tensor_scalar(ogT[:, h, :], xmT[:, h, 0:TOK], pcol[:, CW + h:CW + h + 1],
                                                 pcol[:, CB + h:CB + h + 1], ALU.mult, ALU.add))
                    for j in range(1, 4):
                        c = CW + 4 * j + h
                        ins = nc.vector.scalar_tensor_tensor(ogT[:, h, :], xmT[:, h, j:j + TOK], pcol[:, c:c + 1],
                                                             ogT[:, h, :], ALU.mult, ALU.add)
                        if j < 3 or h < 3:
                            link(ins)
                split_to(C[f"vm.{i}"] + 2)
            ins.then_inc(conv_done, 1)
            split_to(C["og.0"] + 2)
            for i in range(2):
                dve.wait_ge(*freed[f"uqr.{i}"])
            c_, s_ = (a[:, :, :].unsqueeze(2).to_broadcast([P, NT, 5, HALF]) for a in (cos, sin))
            x1, x2 = rin[:, :, :, 0:HALF], rin[:, :, :, HALF:ROPE]
            nc.vector.tensor_tensor(rtmp[:, 0], x2, s_, ALU.mult)
            nc.vector.tensor_tensor(rtmp[:, 1], x2, c_, ALU.mult)
            nc.vector.tensor_tensor(rout[:, :, 0:5, 0:HALF], x1, c_, ALU.mult)
            link(nc.vector.tensor_tensor(rout[:, :, 0:5, HALF:ROPE], x1, s_, ALU.mult))
            nc.vector.tensor_tensor(rout[:, :, 0:5, 0:HALF], rout[:, :, 0:5, 0:HALF], rtmp[:, 0], ALU.subtract)
            link(nc.vector.tensor_tensor(rout[:, :, 0:5, HALF:ROPE], rout[:, :, 0:5, HALF:ROPE], rtmp[:, 1], ALU.add))
            nc.vector.memset(rout[:, :, 5:7, :], 0.0)
            nc.vector.tensor_copy(rout[:, :, 7, :], rout[:, :, 4, :]).then_inc(rope_done, 1)
            attention("mla", FILL["mla"])

            mlstm(dve, link, split_to)
            for i in range(4):
                split_to(C[f"abo.{i}"] + 2)
            post_norm(1)
            outs[0] += 2
            cross(0, 2)
            for s in (3, 4):
                pre_norm(s)
                ffn(s)

            pre_norm(5)
            for name, _, _ in C_COLS[:3]:
                split_to(C[name] + 2)
            for name, a, b in (("ccq", 0, QL), ("cckv", QL, QL + KVL)):
                scale_rows(name, lat[:, :, a:b], lat[:, :, a:b], b - a).then_inc(lat_done, 1)
            mem_lo(1)
            split_to(C["qi.1"] + 2)
            dve.wait_ge(*full("kw"))
            b = bank("kw").rearrange("p (t n) -> p t n", t=NT)
            nc.vector.memset(kk2[:, :, 64:192], 0.0)
            nc.vector.tensor_copy(kk2[:, :, 0:64], b[:, :, 0:64])
            nc.vector.tensor_copy(kk2[:, :, 192:256], b[:, :, 0:64])
            nc.vector.tensor_copy(iw[:, :, :], b[:, :, 64:72]).then_inc(freed["kw"][0], 1)
            dve.wait_ge(*freed["kw"])
            nc.vector.tensor_copy(top8[:, :, :], iw[:, :, :]).then_inc(ki_done, 1)
            dve.wait_ge(ki_done, 1)
            for n in range(8):
                t, i = divmod(n, 4)
                dve.wait_ge(*freed[f"rel{t}.{i}"])
                for j in range(2):
                    acc = cmask[:, t, :] if (i, j) == (0, 0) else score[:, t, :]
                    ins = nc.vector.scalar_tensor_tensor(score[:, t, :], rel[:, n % 2, j, :],
                                                         iw[:, t, 2 * i + j:2 * i + j + 1], acc, ALU.mult, ALU.add)
                    if j == 0:
                        link(ins)
                ins.then_inc(rel_used, 1)
                dve.wait_ge(rel_used, n + 1)
            for t in range(NT):
                for r in range(TOPK // 8):
                    link(nc.vector.max(top8[:, t, :], score[:, t, :]))
                    link(nc.vector.match_replace(score[:, t, :], top8[:, t, :], score[:, t, :], TAKEN))
                link(nc.vector.tensor_scalar(dmask[:, t, :], score[:, t, :], 0.5 * TAKEN, NEG, ALU.is_gt, ALU.mult))
                link(nc.vector.tensor_tensor(dmask[:, t, :], dmask[:, t, :], cmask[:, t, :], ALU.add))
            split_to(C["xk1.0"])
            attention("dsa", FILL["dsa"])
            for i in range(4):
                split_to(C[f"co.{i}"] + 2)
            post_norm(5)
            cross(1, 6)
            pre_norm(7)
            ffn(7)



TWO_PI = (6.28125, float(np.float32(2 * np.pi - 6.28125) // np.float32(2 ** -20) * 2.0 ** -20), 0.0)
TWO_PI = (TWO_PI[0], TWO_PI[1], float(2 * np.pi - TWO_PI[0] - TWO_PI[1]))


def kernel(**inputs):
    import concourse.bacc as bacc
    from concourse.bass_utils import run_bass_kernel_spmd

    nc = bacc.Bacc("TRN2", target_bir_lowering=False, num_devices=1)
    arrays, A = {}, {}
    for name in INS:
        a = np.ascontiguousarray(inputs[name])
        arrays[f"in_{name}"] = a
        A[name] = nc.dram_tensor(f"in_{name}", a.shape, mybir.dt.from_np(a.dtype), kind="ExternalInput").ap()
    out = nc.dram_tensor("out", (1, TOK, D), F32, kind="ExternalOutput").ap()
    build(nc, A, out)
    r = run_bass_kernel_spmd(nc, [arrays], core_ids=[0])
    return r.results[0]["out"]
```
